# Optimizing a Trainium2 kernel written in Bass

```python
import jax, jax.numpy as jnp
from jax import lax
import numpy as np

D_MODEL = 1024
BATCH = 1
SEQ = 256
DEPTH = 2
DEC_BATCH = 1
DEC_SEQ = 256
PAST_LEN = 128

GRID_W = 64
Q_BLOCK = 128
ROPE_THETA = 10000.0
EPS = 1e-6
N_HEADS_A = 8
N_KV_HEADS_A = 2
HEAD_DIM_A = 64
N_HEADS_B = 8
QK_NOPE_DIM = 64
QK_ROPE_DIM = 32
V_DIM_B = 64
Q_LORA = 256
KV_LORA = 128
WIDTH_A = N_HEADS_A * HEAD_DIM_A
WIDTH_B = N_HEADS_B * V_DIM_B
D_MIX = WIDTH_A + WIDTH_B
KV_WIDTH_A = N_KV_HEADS_A * HEAD_DIM_A
D_IN = WIDTH_A + 2 * KV_WIDTH_A + Q_LORA + KV_LORA + QK_ROPE_DIM
D_FF = 2816
CONV_W = 3
N_MOD = 6

kernel_name = "hybrid_gqa_mla_convffn_encoder"

def rms_norm(x, g):
    xf = x.astype(jnp.float32)
    y = xf * lax.rsqrt(jnp.mean(xf * xf, axis=-1, keepdims=True) + EPS)
    return (y * g.astype(jnp.float32)).astype(x.dtype)

def axial_rope_tables(n_tokens, rot_dim):
    rows = n_tokens // GRID_W
    row = jnp.repeat(jnp.arange(rows, dtype=jnp.float32), GRID_W)
    col = jnp.tile(jnp.arange(GRID_W, dtype=jnp.float32), rows)
    quarter = rot_dim // 4
    inv_freq = ROPE_THETA ** (-jnp.arange(quarter, dtype=jnp.float32) / quarter)
    ang = jnp.stack([row, col], axis=-1)[:, :, None] * inv_freq
    return jnp.cos(ang), jnp.sin(ang)

def apply_axial_rope(x, cos, sin):
    d = x.shape[-1]
    q = d // 4
    s_len = x.shape[1]
    bshape = (1, s_len) + (1,) * (x.ndim - 3) + (2, q)
    c = cos.reshape(bshape)
    s = sin.reshape(bshape)
    xr = x.astype(jnp.float32).reshape(x.shape[:-1] + (2, 2, q))
    x1 = xr[..., 0, :]
    x2 = xr[..., 1, :]
    out = jnp.stack([x1 * c - x2 * s, x2 * c + x1 * s], axis=-2)
    return out.reshape(x.shape).astype(x.dtype)

def block_attention(q, k, v):
    b, s, hk, g, dk = q.shape
    dv = v.shape[-1]
    nb = s // Q_BLOCK
    scale = dk ** -0.5
    kf = k.astype(jnp.float32)
    vf = v.astype(jnp.float32)
    qb = q.astype(jnp.float32).reshape(b, nb, Q_BLOCK, hk, g, dk).transpose(1, 0, 2, 3, 4, 5)

    def one_block(qi):
        sc = jnp.einsum('bqhgd,bkhd->bhgqk', qi, kf) * scale
        p = jax.nn.softmax(sc, axis=-1)
        return jnp.einsum('bhgqk,bkhd->bqhgd', p, vf)

    o = lax.map(one_block, qb)
    return o.transpose(1, 0, 2, 3, 4, 5).reshape(b, s, hk, g, dv).astype(q.dtype)

def depthwise_conv_centred(u, w, bias):
    up = jnp.pad(u, ((0, 0), (1, 1), (0, 0)))
    s = u.shape[1]
    return up[:, 0:s] * w[0] + up[:, 1:s + 1] * w[1] + up[:, 2:s + 2] * w[2] + bias

def encoder_layer(x, mod, cos_a, sin_a, cos_b, sin_b, g_attn, w_in, g_q_a, g_k_a, g_cq, w_uq,
                  g_ckv, w_ukv, g_out_a, g_out_b, w_o, g_ffn, w_up, conv_w, conv_b, w_down):
    b, s, _ = x.shape
    shift_a, scale_a, gate_a, shift_f, scale_f, gate_f = jnp.split(mod[:, None, :], N_MOD, axis=-1)

    h = rms_norm(x, g_attn) * (1.0 + scale_a) + shift_a
    proj = h @ w_in
    idx = np.cumsum([WIDTH_A, KV_WIDTH_A, KV_WIDTH_A, Q_LORA, KV_LORA])
    q_a, k_a, v_a, c_q, c_kv, k_r = jnp.split(proj, [int(i) for i in idx], axis=-1)

    q_a = q_a.reshape(b, s, N_KV_HEADS_A, N_HEADS_A // N_KV_HEADS_A, HEAD_DIM_A)
    k_a = k_a.reshape(b, s, N_KV_HEADS_A, HEAD_DIM_A)
    v_a = v_a.reshape(b, s, N_KV_HEADS_A, HEAD_DIM_A)
    q_a = apply_axial_rope(rms_norm(q_a, g_q_a), cos_a, sin_a)
    k_a = apply_axial_rope(rms_norm(k_a, g_k_a), cos_a, sin_a)
    o_a = block_attention(q_a, k_a, v_a).reshape(b, s, WIDTH_A)

    q_b = (rms_norm(c_q, g_cq) @ w_uq).reshape(b, s, N_HEADS_B, QK_NOPE_DIM + QK_ROPE_DIM)
    q_nope, q_rope = jnp.split(q_b, [QK_NOPE_DIM], axis=-1)
    q_rope = apply_axial_rope(q_rope, cos_b, sin_b)
    kv = (rms_norm(c_kv, g_ckv) @ w_ukv).reshape(b, s, N_HEADS_B, QK_NOPE_DIM + V_DIM_B)
    k_nope, v_b = jnp.split(kv, [QK_NOPE_DIM], axis=-1)
    k_rope = apply_axial_rope(k_r, cos_b, sin_b)
    k_rope = jnp.broadcast_to(k_rope[:, :, None, :], (b, s, N_HEADS_B, QK_ROPE_DIM))
    q_full = jnp.concatenate([q_nope, q_rope], axis=-1)[:, :, :, None, :]
    k_full = jnp.concatenate([k_nope, k_rope], axis=-1)
    o_b = block_attention(q_full, k_full, v_b).reshape(b, s, WIDTH_B)

    o = jnp.concatenate([rms_norm(o_a, g_out_a), rms_norm(o_b, g_out_b)], axis=-1) @ w_o
    x = x + gate_a * o

    h = rms_norm(x, g_ffn) * (1.0 + scale_f) + shift_f
    u = depthwise_conv_centred(h @ w_up, conv_w, conv_b)
    val, gate = jnp.split(u, 2, axis=-1)
    y = (jax.nn.silu(gate) * val) @ w_down
    return x + gate_f * y

def encode(x, c, w_ada, b_ada, g_attn, w_in, g_q_a, g_k_a, g_cq, w_uq, g_ckv, w_ukv,
           g_out_a, g_out_b, w_o, g_ffn, w_up, conv_w, conv_b, w_down, g_final):
    n_tokens = x.shape[1]
    cos_a, sin_a = axial_rope_tables(n_tokens, HEAD_DIM_A)
    cos_b, sin_b = axial_rope_tables(n_tokens, QK_ROPE_DIM)
    c_act = jax.nn.silu(c)
    for l in range(DEPTH):
        mod = c_act @ w_ada[l] + b_ada[l]
        x = encoder_layer(x, mod, cos_a, sin_a, cos_b, sin_b, g_attn[l], w_in[l], g_q_a[l], g_k_a[l],
                          g_cq[l], w_uq[l], g_ckv[l], w_ukv[l], g_out_a[l], g_out_b[l], w_o[l],
                          g_ffn[l], w_up[l], conv_w[l], conv_b[l], w_down[l])
    return rms_norm(x, g_final)

def setup_inputs(seed: int = 0) -> dict:
    key = jax.random.key(seed)
    ks = jax.random.split(key, 24)
    f32 = jnp.float32

    def nrm(k, shape, scale):
        return jax.random.normal(k, shape, f32) * scale

    def gain(k, shape):
        return 1.0 + 0.02 * jax.random.normal(k, shape, f32)

    return {
        "x_prompt": nrm(ks[0], (BATCH, SEQ, D_MODEL), 1.0),
        "x_sample": nrm(ks[1], (DEC_BATCH, DEC_SEQ, D_MODEL), 1.0),
        "c_prompt": nrm(ks[2], (BATCH, D_MODEL), 1.0),
        "c_sample": nrm(ks[3], (DEC_BATCH, D_MODEL), 1.0),
        "w_ada": nrm(ks[4], (DEPTH, D_MODEL, N_MOD * D_MODEL), 0.02),
        "b_ada": nrm(ks[5], (DEPTH, N_MOD * D_MODEL), 0.01),
        "g_attn": gain(ks[6], (DEPTH, D_MODEL)),
        "w_in": nrm(ks[7], (DEPTH, D_MODEL, D_IN), D_MODEL ** -0.5),
        "g_q_a": gain(ks[8], (DEPTH, HEAD_DIM_A)),
        "g_k_a": gain(ks[9], (DEPTH, HEAD_DIM_A)),
        "g_cq": gain(ks[10], (DEPTH, Q_LORA)),
        "w_uq": nrm(ks[11], (DEPTH, Q_LORA, N_HEADS_B * (QK_NOPE_DIM + QK_ROPE_DIM)), Q_LORA ** -0.5),
        "g_ckv": gain(ks[12], (DEPTH, KV_LORA)),
        "w_ukv": nrm(ks[13], (DEPTH, KV_LORA, N_HEADS_B * (QK_NOPE_DIM + V_DIM_B)), KV_LORA ** -0.5),
        "g_out_a": gain(ks[14], (DEPTH, WIDTH_A)),
        "g_out_b": gain(ks[15], (DEPTH, WIDTH_B)),
        "w_o": nrm(ks[16], (DEPTH, D_MIX, D_MODEL), D_MIX ** -0.5),
        "g_ffn": gain(ks[17], (DEPTH, D_MODEL)),
        "w_up": nrm(ks[18], (DEPTH, D_MODEL, 2 * D_FF), D_MODEL ** -0.5),
        "conv_w": nrm(ks[19], (DEPTH, CONV_W, 2 * D_FF), CONV_W ** -0.5),
        "conv_b": nrm(ks[20], (DEPTH, 2 * D_FF), 0.01),
        "w_down": nrm(ks[21], (DEPTH, D_FF, D_MODEL), D_FF ** -0.5),
        "g_final": gain(ks[22], (D_MODEL,)),
    }

def reference(x_prompt, x_sample, c_prompt, c_sample, w_ada, b_ada, g_attn, w_in, g_q_a, g_k_a,
              g_cq, w_uq, g_ckv, w_ukv, g_out_a, g_out_b, w_o, g_ffn, w_up, conv_w, conv_b,
              w_down, g_final):
    y_prompt = encode(x_prompt, c_prompt, w_ada, b_ada, g_attn, w_in, g_q_a, g_k_a, g_cq, w_uq,
                      g_ckv, w_ukv, g_out_a, g_out_b, w_o, g_ffn, w_up, conv_w, conv_b, w_down,
                      g_final)
    y_sample = encode(x_sample, c_sample, w_ada, b_ada, g_attn, w_in, g_q_a, g_k_a, g_cq, w_uq,
                      g_ckv, w_ukv, g_out_a, g_out_b, w_o, g_ffn, w_up, conv_w, conv_b, w_down,
                      g_final)
    return (y_prompt, y_sample)


_drawn_inputs = setup_inputs


def setup_inputs(seed=0):
    import zlib

    import numpy as np

    out = dict(_drawn_inputs(seed))
    spreads = {}
    factors = {'g_attn': 8.0,
     'g_q_a': 8.0,
     'g_k_a': 8.0,
     'g_cq': 8.0,
     'g_ckv': 6.842,
     'g_out_a': 7.082,
     'g_out_b': 7.209,
     'g_ffn': 5.532,
     'conv_b': 8.0,
     'g_final': 2.821}
    for name, (base, spread) in spreads.items():
        noise = np.random.default_rng([zlib.crc32(name.encode()), seed]).standard_normal(out[name].shape)
        drawn = base * np.exp(spread * noise) if base else spread * noise
        out[name] = __import__('jax').numpy.asarray(drawn.astype(out[name].dtype))
    for name, factor in factors.items():
        out[name] = (out[name] * factor).astype(out[name].dtype)
    return out
```

```python
from contextlib import ExitStack

import concourse.bass as bass
import numpy as np
from concourse import mybir

F32 = mybir.dt.float32
F32R = mybir.dt.float32r
ALU = mybir.AluOpType
ACT = mybir.ActivationFunctionType
AX_X = mybir.AxisListType.X

P = 128
D_MODEL = 1024
DEPTH = 2
SEQ = 256
NSEQ = 2
T = NSEQ * SEQ
TT = T // P
KD = D_MODEL // P
GRID_W = 64
THETA = 10000.0
EPS = 1e-6
HEADS = 8
HD = 64
KV_HEADS = 2
NOPE = 64
ROT = 32
QK_B = NOPE + ROT
Q_LORA = 256
KV_LORA = 128
D_FF = 2816
FT = D_FF // P
N_MOD = 6

C_CQ = 0
C_CKV = C_CQ + Q_LORA
C_KR = C_CKV + KV_LORA
C_Q = C_KR + ROT
C_K = C_Q + HEADS * HD
C_V = C_K + KV_HEADS * HD
D_IN = C_V + KV_HEADS * HD
CHUNKS = [(C_CQ, 256), (C_CKV, 160), (C_Q, 256), (C_Q + 256, 256), (C_K, 256)]

SLOT = 1024
RING = 4
GROUPS = [8, 8, 6]
S_IN = 0
S_UQ = S_IN + 2 * len(CHUNKS)
S_UKV = S_UQ + 4
S_WO = S_UKV + 2
S_FFN = S_WO + KD
S_UP, S_DOWN = [], []
_at = S_FFN
for _n in GROUPS:
    S_UP.append(_at)
    S_DOWN.append(_at + 2 * _n)
    _at += 2 * _n + KD
SLOTS = _at
ROUNDS = SLOTS // RING
assert SLOTS % RING == 0 and sum(GROUPS) == FT

PC_GATTN = 0
PC_GFFN = PC_GATTN + KD
PC_GOUT = PC_GFFN + KD
PC_GCQ = PC_GOUT + KD
PC_GCKV = PC_GCQ + 2
PC_BADA = PC_GCKV + 1
PC_CW = PC_BADA + N_MOD * KD
PC_CB = PC_CW + 3 * 2 * FT
NPC = PC_CB + 2 * FT
SHIFT_A, SCALE_A, GATE_A, SHIFT_F, SCALE_F, GATE_F = range(N_MOD)

UNITS = [("a", s, p + 4 * g, g == 0) for s in range(NSEQ) for p in range(4) for g in range(2)]
UNITS += [("b", s, h, True) for s in range(NSEQ) for h in range(HEADS)]
NU = len(UNITS)


def plan_banks():
    count, use = [0] * 8, {}

    def take(key, bank):
        use[key] = (bank, count[bank])
        count[bank] += 1

    take("norm1", 6)
    for c in range(len(CHUNKS)):
        for t in range(TT):
            take(("proj", c, t), t)
    for j in range(3):
        take(("lat", j), 4 + j)
    for s in range(4):
        for t in range(TT):
            take(("uq", s, t), t)
    for s in range(2):
        for t in range(TT):
            take(("ukv", s, t), t)
    take("kat", 7)
    pairs = 0
    for i in range(-1, NU + 2):
        if i + 1 < NU and UNITS[i + 1][3]:
            take(("qt", i + 1), 4 + pairs % 2)
            pairs += 1
        if 0 <= i < NU:
            take(("s", i), i % 2)
        if 0 <= i - 1 < NU:
            take(("pt", i - 1), 2 + (i - 1) % 2)
        if 0 <= i - 2 < NU:
            take(("o", i - 2), 6 + i % 2)
    take(("mod", GATE_A), 7)
    for k in range(KD):
        take(("ot", k), k % 4)
    for m in range(KD):
        take(("wo", m), 4 + m % 2)
        if m % 4 == 3:
            take(("mod", SHIFT_F + m // 4), 7)
    take("norm2", 6)
    for g, n in enumerate(GROUPS):
        for i in range(n):
            take(("up", g, i, 0), 2 * (i % 2))
            take(("up", g, i, 1), 2 * (i % 2) + 1)
        take(("mod", (GATE_F + g) % N_MOD), 7)
        for m in range(KD):
            take(("down", g, m), 4 + m % 2)
    return use, count


USE, USES = plan_banks()
PRO7 = 2

ADA_AFTER = {1: 4, 2: 2, 3: 2, 5: 12, 6: 4, 7: 4, 8: 2, 9: 2}
ADA_NEXT = {11: 4, 13: 2, 14: 2, 17: 4, 19: 2, 20: 2}


def encoder_kernel(nc, x_t, c_t, w_slots, ada_slots, params, g_qk, g_fin, tables, ident_d, y_t):
    ctx = ExitStack()
    with ctx:
        base = [16512]

        def sem(name):
            return ctx.enter_context(nc.semaphore(name))

        def put(name, shape, dt=F32, at=None):
            size = 4 * int(np.prod(shape[1:]))
            if at is None:
                at = base[0]
                base[0] += (size + 31) // 32 * 32
            return nc.alloc_sbuf_tensor_at(name, shape, dt, offset=at)

        x = put("x", [P, KD, T])
        at_h = base[0]
        h_hi = put("h_hi", [P, KD, T], F32R)
        h_lo = put("h_lo", [P, KD, T], F32R)
        at_act = base[0]
        a_hi = put("a_hi", [P, 8, T], F32R)
        a_lo = put("a_lo", [P, 8, T], F32R)
        w_raw = put("w_raw", [P, RING, SLOT])
        w_hi = put("w_hi", [P, RING, SLOT], F32R)
        w_lo = put("w_lo", [P, RING, SLOT], F32R)
        ada_raw = put("ada_raw", [P, 4, SLOT])
        ada_acc = put("ada_acc", [P, NSEQ, SLOT])
        at_proj = base[0]
        proj = put("proj", [P, TT, D_IN])
        at_o = base[0]
        o_sb = put("o_sb", [P, TT, D_MODEL])
        rstd = put("rstd", [P, T])
        ssum = put("ssum", [P, T])
        mod = put("mod", [P, N_MOD, KD, NSEQ])
        cact = put("cact", [P, KD, NSEQ])
        par = put("par", [P, DEPTH, NPC])
        gqk = put("gqk", [P, DEPTH, 2, HD])
        gfin = put("gfin", [P, KD])
        tab = put("tab", [P, 2, 2 * (HD + ROT)])
        ident = put("ident", [P, P])
        ones = put("ones", [P, P])
        eps = put("eps", [P, 1])
        cg = put("cg", [P, 2, 2, HD])
        sg_t = put("sg_t", [P, 2, 2, HD])
        st_lat = put("st_lat", [P, 2, 8])
        st_qk = put("st_qk", [P, 2, 40])
        st_o = put("st_o", [P, 2, 8])
        mx = put("mx", [P, NU, 2])
        nmx = put("nmx", [P, NU, 2])
        sme = put("sme", [P, NU, 2])
        rin = put("rin", [P, NU, 2])
        assert base[0] <= nc.sbuf_usable_end, base[0]
        qb = put("qb", [P, TT, HEADS, QK_B], at=at_h)
        kb = put("kb", [P, TT, HEADS, QK_B], at=at_h + 12288)
        vb = put("vb", [P, TT, HEADS * HD], at=at_h + 24576)
        ct_hi = put("ct_hi", [P, 3, T], F32R, at=at_act)
        ct_lo = put("ct_lo", [P, 3, T], F32R, at=at_act + 6144)
        prob = put("prob", [P, 2, 2, SEQ], at=at_act + 12288)
        prob_t = put("prob_t", [P, 2, 2, SEQ], at=at_act + 16384)
        qk_t = put("qk_t", [P, 2, T], at=at_act + 20480)
        ka_t = put("ka_t", [P, T], at=at_act + 24576)
        xn = put("xn", [P, 2, T], at=at_o)
        hf = put("hf", [P, 2, T], at=at_o + 4096)
        root = put("root", [P, T], at=at_o + 8192)
        sq_x = put("sq_x", [P, 2, T], at=at_o + 10240)
        rope_tmp = put("rope_tmp", [P, TT, 640], at=at_o)
        junk = put("junk", [P, 512], at=at_o + 14336)
        u_sb = put("u_sb", [P, 2, 2, T], at=at_proj)
        sil = put("sil", [P, 2, T], at=at_proj + 8192)
        af = put("af", [P, 2, T], at=at_proj + 12288)
        ps = ctx.enter_context(nc.psum_tensor("ps", [P, 8, 512], F32))

        cos_a = tab[:, 0, 0:2 * HD].rearrange("p (e d) -> p e d", e=2)
        sin_a = tab[:, 1, 0:2 * HD].rearrange("p (e d) -> p e d", e=2)
        cos_b = tab[:, 0, 2 * HD:].rearrange("p (e d) -> p e d", e=2)
        sin_b = tab[:, 1, 2 * HD:].rearrange("p (e d) -> p e d", e=2)

        loaded = sem("loaded")
        raw_landed = [sem(f"raw_landed{j}") for j in range(RING)]
        raw_free = sem("raw_free")
        split_begun = sem("split_begun")
        split_done = sem("split_done")
        slot_free = sem("slot_free")
        ada_landed = [sem(f"ada_landed{j}") for j in range(4)]
        ada_used = sem("ada_used")
        acc_ready = sem("acc_ready")
        mod_ready = sem("mod_ready")
        c_ready = sem("c_ready")
        full = [sem(f"bank_full{b}") for b in range(8)]
        free = [sem(f"bank_free{b}") for b in range(8)]
        const_ready = sem("const_ready")
        ssum_ready = sem("ssum_ready")
        root_ready = sem("root_ready")
        xn_ready = sem("xn_ready")
        h_hi_ready = sem("h_hi_ready")
        h_ready = sem("h_ready")
        sq_q = sem("sq_q")
        lat_sq = sem("lat_sq")
        lat_ready = sem("lat_ready")
        ct_hi_ready = sem("ct_hi_ready")
        ct_ready = sem("ct_ready")
        qk_sq = sem("qk_sq")
        qk_ms = sem("qk_ms")
        qk_root = sem("qk_root")
        qk_ready = sem("qk_ready")
        ka_ready = sem("ka_ready")
        b_ready = sem("b_ready")
        qt_ready = sem("qt_ready")
        max_ready = sem("max_ready")
        exp_ready = sem("exp_ready")
        pt_ready = sem("pt_ready")
        o_root = sem("o_root")
        o_ready = sem("o_ready")
        ot_hi_ready = sem("ot_hi_ready")
        ot_ready = sem("ot_ready")
        x_upd = sem("x_upd")
        sq_ready = sem("sq_ready")
        mid_tap = sem("mid_tap")
        taps_done = sem("taps_done")
        sil_ready = sem("sil_ready")
        af_ready = sem("af_ready")
        a_hi_ready = sem("a_hi_ready")
        a_ready = sem("a_ready")
        y_done = sem("y_done")
        stored = sem("stored")

        def bank(key):
            return USE[key][0]

        def n_use(L, key):
            b, n = USE[key]
            return L * USES[b] + n + (PRO7 if b == 7 else 0)

        def wait_full(eng, L, key, plus=0):
            eng.wait_ge(full[bank(key)], n_use(L, key) + 1 + plus)

        def wait_free(eng, L, key, plus=0):
            n = n_use(L, key) + plus
            if type(n) is not int or n > 0:
                eng.wait_ge(free[bank(key)], n)

        block = ctx.enter_context(nc.Block())

        N_LOADS = 8

        @block.sync
        def _(sp):
            def load_ada(n_vec, kt):
                sp.wait_ge(ada_used, 8 * n_vec + kt + 1)
                sp.dma_start(ada_raw[:, kt % 4, :], ada_slots[8 * n_vec + kt]).then_inc(ada_landed[kt % 4], 16)

            def load_round(L, r):
                for j in range(RING):
                    sp.wait_ge(raw_free, L * SLOTS + RING * r + j + 1)
                    sp.dma_start(w_raw[:, j, :], w_slots[L * SLOTS + RING * r + j]).then_inc(raw_landed[j], 16)

            sp.dma_start(cact[:], c_t).then_inc(loaded, 16)
            sp.dma_start(par[:], params).then_inc(loaded, 16)
            for kt in range(4):
                load_ada(0, kt)
            for k in range(2):
                sp.dma_start(x[:, 4 * k:4 * k + 4, :], x_t[:, 4 * k:4 * k + 4, :]).then_inc(loaded, 16)
            sp.dma_start(gqk[:], g_qk).then_inc(loaded, 16)
            sp.dma_start(gfin[:], g_fin).then_inc(loaded, 16)
            sp.dma_start(tab[:], tables).then_inc(loaded, 16)
            sp.dma_start(ident[:], ident_d).then_inc(loaded, 16)
            for kt in range(4, 8):
                load_ada(0, kt)
            for kt in range(8):
                load_ada(1, kt)
            for L in range(DEPTH):
                a = [8 * (N_MOD * L + GATE_A)]
                for r in range(ROUNDS):
                    load_round(L, r)
                    n = ADA_AFTER.get(r, 0) + (ADA_NEXT.get(r, 0) if L + 1 < DEPTH else 0)
                    for _ in range(n):
                        load_ada(a[0] // 8, a[0] % 8)
                        a[0] += 1
            for k in range(KD):
                sp.wait_ge(y_done, k + 1)
                sp.dma_start(y_t[:, k, :], x[:, k, :]).then_inc(stored, 16)
            sp.wait_ge(stored, 16 * KD)

        @block.gpsimd
        def _(pool):
            nc.gpsimd.memset(ones[:], 1.0)
            nc.gpsimd.memset(eps[:], EPS)
            nc.gpsimd.drain()
            pool.sem_inc(const_ready, 1)
            pool.sem_inc(raw_free, RING)
            with pool.Fori(0, DEPTH * ROUNDS) as r:
                for j in range(RING):
                    pool.wait_ge(slot_free, RING * r + j + 1)
                    pool.wait_ge(raw_landed[j], 16 * r + 16)
                    pool.sem_inc(split_begun, 1)
                    nc.gpsimd.tensor_copy(w_hi[:, j, :], w_raw[:, j, :])
                    nc.gpsimd.drain()
                    nc.gpsimd.tensor_tensor(w_lo[:, j, :], w_raw[:, j, :], w_hi[:, j, :].bitcast(F32),
                                            ALU.subtract)
                    nc.gpsimd.drain()
                    pool.sem_inc(raw_free, 1)
                    pool.sem_inc(split_done, 1)

        @block.tensor
        def _(pe):
            mm = nc.tensor.matmul
            pe.sem_inc(slot_free, RING - 1)

            def slot(L, s):
                pe.wait_ge(split_done, L * SLOTS + s + 1)
                return s % RING

            def product(out, stat, mov, first, last, release=0):
                hh = mm(out, stat[0], mov[0], start=first, stop=False)
                hl = mm(out, stat[0], mov[1], start=False, stop=False)
                if release >= 1:
                    hh.then_inc(slot_free, 1)
                if release >= 2:
                    hl.then_inc(slot_free, 1)
                return mm(out, stat[1], mov[0], start=False, stop=last)

            def sum_mod(L, v, n_vec):
                pe.wait_ge(acc_ready, n_vec + 1)
                if L is None:
                    b = 7
                    if v:
                        pe.wait_ge(free[7], v)
                else:
                    wait_free(pe, L, ("mod", v))
                    b = 7
                for j in range(KD):
                    for s in range(NSEQ):
                        last = mm(ps[:, b, 2 * j + s:2 * j + s + 1], ada_acc[:, s, P * j:P * j + P], ones[:, 0:1],
                                  start=True, stop=True)
                last.then_inc(full[b], 1)

            def norm_sum(L, which, n):
                pe.wait_ge(ssum_ready, n + 1)
                wait_free(pe, L, which)
                mm(ps[:, 6, :], ones[:], ssum[:], start=True, stop=True).then_inc(full[6], 1)

            pe.wait_ge(const_ready, 1)
            pe.wait_ge(loaded, 16 * N_LOADS)
            for v in range(2):
                sum_mod(None, v, v)

            for L in range(DEPTH):
                norm_sum(L, "norm1", 2 * L)
                for c, (col, width) in enumerate(CHUNKS):
                    halves = [0, 0]

                    def part(k, t, first, last, release=0):
                        j = halves[k // 4]
                        w = [r[:, j, (k % 4) * width:(k % 4 + 1) * width] for r in (w_hi, w_lo)]
                        st = [r[:, k, t * P:t * P + P] for r in (h_hi, h_lo)]
                        return product(ps[:, t, 0:width], st, w, first, last, release)

                    if c == 0:
                        for k in range(KD):
                            if k % 4 == 0:
                                halves[k // 4] = slot(L, S_IN + k // 4)
                            pe.wait_ge(h_ready, 16 * L + k + 1)
                            for t in range(TT):
                                if k == 0:
                                    wait_free(pe, L, ("proj", c, t))
                                last = part(k, t, k == 0, k == KD - 1, int(k == 0 and t == 0))
                                if k == KD - 1:
                                    last.then_inc(full[t], 1)
                    else:
                        for t in range(TT):
                            wait_free(pe, L, ("proj", c, t))
                            for k in range(KD):
                                if t == 0 and k % 4 == 0:
                                    halves[k // 4] = slot(L, S_IN + 2 * c + k // 4)
                                last = part(k, t, k == 0, k == KD - 1, 2 * int(k == 0 and t == 0))
                            last.then_inc(full[t], 1)
                pe.wait_ge(lat_ready, L + 1)
                for j in range(3):
                    wait_free(pe, L, ("lat", j))
                    for t in range(TT):
                        last = nc.tensor.transpose(ps[:, 4 + j, t * P:t * P + P], proj[:, t, j * P:j * P + P], ident[:])
                    last.then_inc(full[4 + j], 1)
                width = 2 * QK_B
                for s in range(4):
                    j = slot(L, S_UQ + s)
                    if s == 0:
                        pe.wait_ge(ct_ready, 3 * L + 2)
                    for t in range(TT):
                        wait_free(pe, L, ("uq", s, t))
                        for k in range(2):
                            last = product(ps[:, t, 0:width], [r[:, k, t * P:t * P + P] for r in (ct_hi, ct_lo)],
                                           [r[:, j, k * width:(k + 1) * width] for r in (w_hi, w_lo)], k == 0, k == 1,
                                           (1 + int(s == 0)) * int(k == 0 and t == 0))
                        last.then_inc(full[t], 1)
                pe.wait_ge(ct_ready, 3 * L + 3)
                for s in range(2):
                    j = slot(L, S_UKV + s)
                    for t in range(TT):
                        wait_free(pe, L, ("ukv", s, t))
                        product(ps[:, t, :], [r[:, 2, t * P:t * P + P] for r in (ct_hi, ct_lo)],
                                [r[:, j, 0:512] for r in (w_hi, w_lo)], True, True, int(t == 0)).then_inc(full[t], 1)
                pe.wait_ge(qk_ready, L + 1)
                wait_free(pe, L, "kat")
                for t in range(TT):
                    last = nc.tensor.transpose(ps[:, 7, t * P:t * P + P], proj[:, t, C_K:C_K + P], ident[:])
                last.then_inc(full[7], 1)
                for i in range(-1, NU + 2):
                    if i + 1 < NU and UNITS[i + 1][3]:
                        group, s, h, _ = UNITS[i + 1]
                        b = bank(("qt", i + 1))
                        wait_free(pe, L, ("qt", i + 1))
                        if group == "b" and UNITS[i][0] == "a":
                            pe.wait_ge(b_ready, L + 1)
                        for q in range(2):
                            if group == "a":
                                last = nc.tensor.transpose(ps[:, b, q * P:q * P + P],
                                                           proj[:, 2 * s + q, C_Q + h * P:C_Q + h * P + P], ident[:])
                            else:
                                nc.tensor.transpose(ps[0:QK_B, b, q * P:q * P + P], qb[:, 2 * s + q, h, :], ident[:])
                                last = nc.tensor.transpose(ps[0:QK_B, b, SEQ + q * P:SEQ + q * P + P],
                                                           kb[:, 2 * s + q, h, :], ident[:])
                        last.then_inc(full[b], 1)
                    if 0 <= i < NU:
                        group, s, h, _ = UNITS[i]
                        wait_free(pe, L, ("s", i))
                        pe.wait_ge(qt_ready, QT_DONE(L, i))
                        if i == 0:
                            pe.wait_ge(ka_ready, L + 1)
                        buf = QT_BUF(i)
                        for q in range(2):
                            if group == "a":
                                o = 64 * (h // 4)
                                st, mv = qk_t[o:o + 64, buf, q * P:q * P + P], ka_t[o:o + 64, s * SEQ:(s + 1) * SEQ]
                            else:
                                st, mv = qk_t[0:QK_B, buf, q * P:q * P + P], qk_t[0:QK_B, buf, SEQ:2 * SEQ]
                            last = mm(ps[:, i % 2, q * SEQ:(q + 1) * SEQ], st, mv, start=True, stop=True)
                        last.then_inc(full[i % 2], 1)
                    if 0 <= i - 1 < NU:
                        u = i - 1
                        wait_free(pe, L, ("pt", u))
                        pe.wait_ge(exp_ready, L * NU + u + 1)
                        for q in range(2):
                            for k in range(2):
                                last = nc.tensor.transpose(
                                    ps[:, 2 + u % 2, k * SEQ + q * P:k * SEQ + q * P + P],
                                    prob[:, u % 2, q, k * P:k * P + P], ident[:])
                        last.then_inc(full[2 + u % 2], 1)
                    if 0 <= i - 2 < NU:
                        u = i - 2
                        group, s, h, _ = UNITS[u]
                        b = bank(("o", u))
                        wait_free(pe, L, ("o", u))
                        pe.wait_ge(pt_ready, L * NU + u + 1)
                        for q in range(2):
                            for k in range(2):
                                if group == "a":
                                    v = proj[:, 2 * s + k, C_V + HD * (h // 4):C_V + HD * (h // 4) + HD]
                                else:
                                    v = vb[:, 2 * s + k, h * HD:(h + 1) * HD]
                                last = mm(ps[:, b, q * HD:(q + 1) * HD], prob_t[:, u % 2, k, q * P:q * P + P], v,
                                          start=(k == 0), stop=(k == 1))
                        last.then_inc(full[b], 1)
                sum_mod(L, GATE_A, N_MOD * L + GATE_A)
                pe.wait_ge(o_ready, L + 1)
                for k in range(KD):
                    wait_free(pe, L, ("ot", k))
                    for t in range(TT):
                        last = nc.tensor.transpose(ps[:, k % 4, t * P:t * P + P], o_sb[:, t, k * P:k * P + P], ident[:])
                    last.then_inc(full[k % 4], 1)
                for m in range(KD):
                    j = slot(L, S_WO + m)
                    wait_free(pe, L, ("wo", m))
                    for k in range(KD):
                        if m == 0:
                            pe.wait_ge(ot_ready, KD * L + k + 1)
                        last = product(ps[:, 4 + m % 2, :], [r[:, j, k * P:k * P + P] for r in (w_hi, w_lo)],
                                       [r[:, k, :] for r in (h_hi, h_lo)], k == 0, k == KD - 1, int(k == 0))
                    last.then_inc(full[4 + m % 2], 1)
                    if m % 4 == 3:
                        sum_mod(L, SHIFT_F + m // 4, N_MOD * L + SHIFT_F + m // 4)
                norm_sum(L, "norm2", 2 * L + 1)
                for g, n in enumerate(GROUPS):
                    if g == 0:
                        pe.wait_ge(h_ready, 16 * L + 16)
                    with pe.Fori(0, n // 2) as it:
                        for e in range(2):
                            for half in range(2):
                                key = ("up", g, e, half)
                                pe.wait_ge(split_done, 4 * it + (L * SLOTS + S_UP[g] + 2 * e + half + 1))
                                wait_free(pe, L, key, it)
                                j = (S_UP[g] + 2 * e + half) % RING
                                for k in range(KD):
                                    last = product(ps[:, bank(key), :],
                                                   [r[:, j, k * P:k * P + P] for r in (w_hi, w_lo)],
                                                   [r[:, k, :] for r in (h_hi, h_lo)], k == 0, k == KD - 1, int(k == 0))
                                last.then_inc(full[bank(key)], 1)
                    v = (GATE_F + g) % N_MOD
                    if g == 0 or L + 1 < DEPTH:
                        sum_mod(L, v, N_MOD * L + GATE_F + g)
                    with pe.Fori(0, KD // 4) as it:
                        for e in range(4):
                            key = ("down", g, e)
                            pe.wait_ge(split_done, 4 * it + (L * SLOTS + S_DOWN[g] + e + 1))
                            wait_free(pe, L, key, 2 * it)
                            j = (S_DOWN[g] + e) % RING
                            for k in range(n):
                                if e == 0:
                                    pe.wait_ge(a_ready, L * FT + sum(GROUPS[:g]) + k + 1)
                                last = product(ps[:, bank(key), :],
                                               [r[:, j, k * P:k * P + P] for r in (w_hi, w_lo)],
                                               [r[:, k, :] for r in (a_hi, a_lo)], k == 0, k == n - 1, int(k == 0))
                            last.then_inc(full[bank(key)], 1)
            pe.wait_ge(ssum_ready, 2 * DEPTH + 1)
            pe.wait_ge(free[6], DEPTH * USES[6])
            mm(ps[:, 6, :], ones[:], ssum[:], start=True, stop=True).then_inc(full[6], 1)

        @block.scalar
        def _(act):
            A = nc.scalar.activation

            def root_of_norm(n_full, n):
                act.wait_ge(full[6], n_full)
                A(root[:], ps[:, 6, :], ACT.Sqrt, bias=eps[:], scale=1.0 / D_MODEL)
                nc.scalar.drain()
                act.sem_inc(free[6], 1)
                act.sem_inc(root_ready, 1)

            def make_h(L, half, gain):
                sh, sc = (SHIFT_A, SCALE_A) if half == 0 else (SHIFT_F, SCALE_F)
                act.wait_ge(mod_ready, N_MOD * L + sc + 1)
                for k in range(KD):
                    n = 16 * L + 8 * half + k
                    act.wait_ge(xn_ready, n + 1)
                    if n >= 2:
                        act.wait_ge(h_ready, n - 1)
                    for s in range(NSEQ):
                        c = slice(s * SEQ, (s + 1) * SEQ)
                        A(hf[:, k % 2, c], xn[:, k % 2, c], ACT.Identity, bias=mod[:, sh, k, s:s + 1],
                          scale=mod[:, sc, k, s:s + 1])
                    nc.scalar.drain()
                    nc.scalar.copy(h_hi[:, k, :], hf[:, k % 2, :]).then_inc(h_hi_ready, 1)

            def square_x(k, n):
                A(sq_x[:, n % 2, :], x[:, k, :], ACT.Square).then_inc(sq_ready, 1)

            act.wait_ge(loaded, 16 * N_LOADS)
            act.wait_ge(const_ready, 1)
            A(cact[:], cact[:], ACT.Silu).then_inc(c_ready, 1)
            for k in range(KD):
                if k >= 2:
                    act.wait_ge(sq_q, k - 1)
                square_x(k, k)

            for L in range(DEPTH):
                root_of_norm(L * USES[6] + USE["norm1"][1] + 1, 2 * L)
                make_h(L, 0, None)
                for c, (col, width) in enumerate(CHUNKS):
                    for t in range(TT):
                        wait_full(act, L, ("proj", c, t))
                        nc.scalar.copy(proj[:, t, col:col + width], ps[:, t, 0:width]).then_inc(free[t], 1)
                    if c == 1:
                        nc.scalar.drain()
                        for t in range(TT):
                            A(junk[:, 0:Q_LORA], proj[:, t, C_CQ:C_CQ + Q_LORA], ACT.Square, scale=Q_LORA ** -0.5,
                              accum_out=st_lat[:, 0, t:t + 1])
                            nc.scalar.drain()
                            A(junk[:, 0:KV_LORA], proj[:, t, C_CKV:C_CKV + KV_LORA], ACT.Square,
                              scale=KV_LORA ** -0.5, accum_out=st_lat[:, 0, 4 + t:5 + t])
                            nc.scalar.drain()
                        A(st_lat[:, 1, :], st_lat[:, 0, :], ACT.Sqrt, bias=eps[:]).then_inc(lat_sq, 1)
                nc.scalar.drain()
                A(rope_tmp[:], proj[:, :, C_Q:C_V], ACT.Square).then_inc(qk_sq, 1)
                act.wait_ge(qk_ms, L + 1)
                A(st_qk[:, 1, :], st_qk[:, 0, :], ACT.Sqrt, bias=eps[:], scale=1.0 / HD).then_inc(qk_root, 1)
                for j in range(3):
                    wait_full(act, L, ("lat", j))
                    A(ct_hi[:, j, :], ps[:, 4 + j, :], ACT.Identity,
                      scale=par[:, L, PC_GCQ + j:PC_GCQ + j + 1]).then_inc(ct_hi_ready, 1)
                for s in range(4):
                    for t in range(TT):
                        wait_full(act, L, ("uq", s, t))
                        nc.scalar.copy(qb[:, t, 2 * s:2 * s + 2, :],
                                       ps[:, t, 0:2 * QK_B].rearrange("p (h d) -> p h d", h=2)).then_inc(free[t], 1)
                for s in range(2):
                    for t in range(TT):
                        wait_full(act, L, ("ukv", s, t))
                        if s == 0:
                            nc.scalar.copy(kb[:, t, :, 0:NOPE],
                                           ps[:, t, :].rearrange("p (h d) -> p h d", h=HEADS)).then_inc(free[t], 1)
                        else:
                            nc.scalar.copy(vb[:, t, :], ps[:, t, :]).then_inc(free[t], 1)
                wait_full(act, L, "kat")
                nc.scalar.copy(ka_t[:], ps[:, 7, :])
                nc.scalar.drain()
                act.sem_inc(free[7], 1)
                act.sem_inc(ka_ready, 1)
                for i in range(-1, NU):
                    if i + 1 < NU and UNITS[i + 1][3]:
                        u = i + 1
                        b, buf = bank(("qt", u)), QT_BUF(u)
                        wait_full(act, L, ("qt", u))
                        last_reader = QT_LAST_READER(u)
                        if last_reader is not None:
                            wait_full(act, L, ("s", last_reader))
                        if UNITS[u][0] == "a":
                            nc.scalar.copy(qk_t[:, buf, 0:SEQ], ps[:, b, 0:SEQ])
                        else:
                            nc.scalar.copy(qk_t[0:QK_B, buf, :], ps[0:QK_B, b, :])
                        nc.scalar.drain()
                        act.sem_inc(free[b], 1)
                        act.sem_inc(qt_ready, 1)
                    if i >= 0:
                        d = HD if UNITS[i][0] == "a" else QK_B
                        act.wait_ge(max_ready, L * NU + i + 1)
                        if i >= 2:
                            wait_full(act, L, ("pt", i - 2))
                        for q in range(2):
                            A(prob[:, i % 2, q, :], ps[:, i % 2, q * SEQ:(q + 1) * SEQ], ACT.Exp,
                              bias=nmx[:, i, q:q + 1], scale=d ** -0.5, accum_out=sme[:, i, q:q + 1])
                        nc.scalar.drain()
                        act.sem_inc(free[i % 2], 1)
                        act.sem_inc(exp_ready, 1)
                act.wait_ge(free[bank(("o", NU - 1))], n_use(L, ("o", NU - 1)) + 1)
                for t in range(TT):
                    for g in range(2):
                        A(prob[:, 0, :, :], o_sb[:, t, 512 * g:512 * g + 512].rearrange("p (a b) -> p a b", a=2),
                          ACT.Square, scale=512 ** -0.5, accum_out=st_o[:, 0, 2 * t + g:2 * t + g + 1])
                        nc.scalar.drain()
                A(st_o[:, 1, :], st_o[:, 0, :], ACT.Sqrt, bias=eps[:]).then_inc(o_root, 1)
                for k in range(KD):
                    wait_full(act, L, ("ot", k))
                    A(h_hi[:, k, :], ps[:, k % 4, :], ACT.Identity,
                      scale=par[:, L, PC_GOUT + k:PC_GOUT + k + 1]).then_inc(ot_hi_ready, 1)
                for m in range(KD):
                    n = KD + 2 * KD * L + m
                    act.wait_ge(x_upd, 2 * KD * L + m + 1)
                    act.wait_ge(sq_q, n - 1)
                    square_x(m, n)
                root_of_norm(L * USES[6] + USE["norm2"][1] + 1, 2 * L + 1)
                make_h(L, 1, None)
                for g, n in enumerate(GROUPS):
                    first = sum(GROUPS[:g])
                    with act.Fori(0, n // 2) as it:
                        for e in range(2):
                            tile = L * FT + first + e
                            for half in range(2):
                                ft = 2 * it + (half * FT + first + e)
                                key = ("up", g, e, half)
                                act.wait_ge(full[bank(key)], it + (n_use(L, key) + 1))
                                A(u_sb[:, e, half, :], ps[:, bank(key), :], ACT.Identity,
                                  bias=par[:, L, bass.ds(ft + PC_CB, 1)],
                                  scale=par[:, L, bass.ds(ft + (PC_CW + 2 * FT), 1)]).then_inc(mid_tap, 1)
                            act.wait_ge(taps_done, 2 * it + (tile + 1))
                            A(sil[:, e, :], u_sb[:, e, 1, :], ACT.Silu).then_inc(sil_ready, 1)
                            act.wait_ge(af_ready, 2 * it + (tile + 1))
                            nc.scalar.copy(a_hi[:, bass.ds(2 * it + e, 1), :], af[:, e:e + 1, :]).then_inc(a_hi_ready, 1)
                for m in range(KD):
                    n = KD + 2 * KD * L + KD + m
                    act.wait_ge(x_upd, 2 * KD * L + KD + m + 1)
                    act.wait_ge(sq_q, n - 1)
                    square_x(m, n)
            root_of_norm(DEPTH * USES[6] + 1, 2 * DEPTH)

        @block.vector
        def _(dve):
            V = nc.vector

            def ada_start(n_vec):
                if n_vec >= 1:
                    L, v = divmod(n_vec - 1, N_MOD)
                    if n_vec - 1 < 2:
                        dve.wait_ge(full[7], n_vec)
                    else:
                        wait_full(dve, L if v >= 2 else L - 1, ("mod", v))
                V.memset(ada_acc[:], 0.0)
                V.drain()

            def ada_slot(n_vec, kt, plus=None):
                dve.wait_ge(ada_landed[kt % 4], 16 * (2 * n_vec + kt // 4 + 1))
                for s in range(NSEQ):
                    V.scalar_tensor_tensor(out=ada_acc[:, s, :], in0=ada_raw[:, kt % 4, :], scalar=cact[:, kt, s:s + 1],
                                           in1=ada_acc[:, s, :], op0=ALU.mult, op1=ALU.add)
                V.drain()
                dve.sem_inc(ada_used, 1)
                if kt == KD - 1:
                    dve.sem_inc(acc_ready, 1)

            def ada_finish(n_vec):
                L, v = divmod(n_vec, N_MOD)
                if n_vec < 2:
                    dve.wait_ge(full[7], n_vec + 1)
                else:
                    wait_full(dve, L if v >= 2 else L - 1, ("mod", v))
                bias = par[:, L, PC_BADA + v * KD:PC_BADA + (v + 1) * KD]
                V.tensor_tensor(mod[:, v, :, :], ps[:, 7, 0:2 * KD].rearrange("p (k s) -> p k s", s=2),
                                bias.rearrange("p (k o) -> p k o", o=1).broadcast_to([P, KD, NSEQ]), ALU.add)
                V.drain()
                if v in (SCALE_A, SCALE_F):
                    g0 = PC_GATTN if v == SCALE_A else PC_GFFN
                    V.tensor_scalar(mod[:, v, :, :], mod[:, v, :, :], 1.0, None, ALU.add)
                    V.drain()
                    V.tensor_tensor(mod[:, v, :, :], mod[:, v, :, :],
                                    par[:, L, g0:g0 + KD].rearrange("p (k o) -> p k o", o=1).broadcast_to([P, KD, NSEQ]),
                                    ALU.mult)
                    V.drain()
                dve.sem_inc(free[7], 1)
                dve.sem_inc(mod_ready, 1)

            def normalise(L, half):
                dve.wait_ge(root_ready, 2 * L + half + 1)
                V.reciprocal(rstd[:], root[:])
                V.drain()

                def lo(k):
                    n = 16 * L + 8 * half + k
                    dve.wait_ge(h_hi_ready, n + 1)
                    V.tensor_tensor(h_lo[:, k, :], hf[:, k % 2, :], h_hi[:, k, :].bitcast(F32),
                                    ALU.subtract).then_inc(h_ready, 1)

                for k in range(KD):
                    V.tensor_tensor(xn[:, k % 2, :], x[:, k, :], rstd[:], ALU.mult).then_inc(xn_ready, 1)
                    if k >= 1:
                        lo(k - 1)
                lo(KD - 1)

            def add_square(n):
                dve.wait_ge(sq_ready, n + 1)
                V.tensor_tensor(ssum[:], ssum[:], sq_x[:, n % 2, :], ALU.add)
                V.drain()
                dve.sem_inc(sq_q, 1)

            def update_x(L, key, k, v, plus=0, done=True):
                wait_full(dve, L, key, plus)
                for s in range(NSEQ):
                    c = slice(s * SEQ, (s + 1) * SEQ)
                    if type(k) is int:
                        xs, gate = x[:, k, c], mod[:, v, k, s:s + 1]
                    else:
                        xs, gate = x[:, bass.ds(k, 1), c], mod[:, v, bass.ds(k, 1), s]
                    V.scalar_tensor_tensor(out=xs, in0=ps[:, bank(key), c], scalar=gate, in1=xs,
                                           op0=ALU.mult, op1=ALU.add)
                V.drain()
                dve.sem_inc(free[bank(key)], 1)
                if done:
                    dve.sem_inc(x_upd, 1)

            def rope_part(out, src, table):
                V.tensor_tensor(out, src, table, ALU.mult)

            dve.sem_inc(ada_used, 4)
            dve.wait_ge(c_ready, 1)
            dve.wait_ge(const_ready, 1)
            ada_start(0)
            for kt in range(KD):
                ada_slot(0, kt)
            V.memset(ssum[:], 0.0)
            V.drain()
            for k in range(KD):
                add_square(k)
            dve.sem_inc(ssum_ready, 1)
            ada_start(1)
            for kt in range(KD):
                ada_slot(1, kt)
                if kt == 3:
                    ada_finish(0)
            ada_finish(1)

            for L in range(DEPTH):
                n0 = N_MOD * L
                normalise(L, 0)
                for w in range(2):
                    g = gqk[:, L, w:w + 1, :]
                    V.tensor_tensor(cg[:, w], cos_a, g.broadcast_to([P, 2, HD]), ALU.mult)
                    for hf_ in range(2):
                        def quarter(ap, f):
                            return ap.rearrange("p e (s f d) -> p e s f d", s=2, f=2)[:, :, :, f, :]
                        V.tensor_tensor(quarter(sg_t[:, w], hf_), quarter(sin_a, hf_),
                                        quarter(g, 1 - hf_).broadcast_to([P, 2, 2, HD // 4]), ALU.mult)
                ada_start(n0 + GATE_A)
                for kt in range(4):
                    ada_slot(n0 + GATE_A, kt)
                dve.wait_ge(lat_sq, L + 1)
                V.reciprocal(st_lat[:, 0, :], st_lat[:, 1, :])
                V.drain()
                for t in range(TT):
                    V.tensor_scalar(proj[:, t, C_CQ:C_CKV], proj[:, t, C_CQ:C_CKV], st_lat[:, 0, t:t + 1], None, ALU.mult)
                    V.tensor_scalar(proj[:, t, C_CKV:C_KR], proj[:, t, C_CKV:C_KR], st_lat[:, 0, 4 + t:5 + t], None,
                                    ALU.mult)
                V.drain()
                dve.sem_inc(lat_ready, 1)
                for kt in range(4, KD):
                    ada_slot(n0 + GATE_A, kt)
                dve.wait_ge(qk_sq, L + 1)
                V.tensor_reduce(out=st_qk[:, 0, :], in_=rope_tmp[:].rearrange("p t (h d) -> p (t h) d", d=HD), op=ALU.add,
                                axis=AX_X)
                V.drain()
                dve.sem_inc(qk_ms, 1)
                heads = [(0, 0, HEADS), (1, HEADS, KV_HEADS)]
                for w, h0, nh in heads:
                    for t in range(TT):
                        for f in range(2):
                            def view(ap, f):
                                return ap[:, h0 * HD:(h0 + nh) * HD].rearrange(
                                    "p (h s f d) -> p h s f d", s=2, f=2, d=HD // 4)[:, :, :, f, :]
                            tb = sg_t[:, w, t % 2:t % 2 + 1, :].rearrange("p o (s f d) -> p o s f d", s=2, f=2)[:, :, :, f, :]
                            V.tensor_tensor(view(rope_tmp[:, t, :], f), view(proj[:, t, C_Q:C_V], 1 - f),
                                            tb.broadcast_to([P, nh, 2, HD // 4]), ALU.mult)
                V.drain()
                for w, h0, nh in heads:
                    for t in range(TT):
                        xv = proj[:, t, C_Q + h0 * HD:C_Q + (h0 + nh) * HD].rearrange("p (h d) -> p h d", d=HD)
                        V.tensor_tensor(xv, xv, cg[:, w, t % 2:t % 2 + 1, :].broadcast_to([P, nh, HD]), ALU.mult)
                V.drain()
                qk = proj[:, :, C_Q:C_V]
                V.tensor_tensor(qk, qk, rope_tmp[:], ALU.add)
                dve.wait_ge(qk_root, L + 1)
                V.reciprocal(st_qk[:, 0, :], st_qk[:, 1, :])
                V.drain()
                qk4 = qk.rearrange("p t (h d) -> p t h d", d=HD)
                V.tensor_tensor(qk4, qk4, st_qk[:, 0, :].rearrange("p (t h o) -> p t h o", t=TT, o=1).broadcast_to(
                    [P, TT, HEADS + KV_HEADS, HD]), ALU.mult)
                V.drain()
                dve.sem_inc(qk_ready, 1)
                for j in range(3):
                    dve.wait_ge(ct_hi_ready, 3 * L + j + 1)
                    V.scalar_tensor_tensor(out=ct_lo[:, j, :], in0=ps[:, 4 + j, :],
                                           scalar=par[:, L, PC_GCQ + j:PC_GCQ + j + 1],
                                           in1=ct_hi[:, j, :].bitcast(F32), op0=ALU.mult, op1=ALU.subtract)
                    V.drain()
                    dve.sem_inc(free[4 + j], 1)
                    dve.sem_inc(ct_ready, 1)
                kr = proj[:, :, C_KR:C_KR + ROT]
                kt_tmp = rope_tmp[:, :, 0:ROT]

                def rot_view(ap, f):
                    return ap.rearrange("p t (s f d) -> p t s f d", s=2, f=2)[:, :, :, f, :]

                for e in range(2):
                    for f in range(2):
                        tb = sin_b[:, e:e + 1, :]
                        V.tensor_tensor(rot_view(kt_tmp[:, e::2, :], f), rot_view(kr[:, e::2, :], 1 - f),
                                        rot_view(tb, f).broadcast_to([P, 2, 2, ROT // 4]), ALU.mult)
                V.drain()
                for e in range(2):
                    V.tensor_tensor(kr[:, e::2, :], kr[:, e::2, :], cos_b[:, e:e + 1, :].broadcast_to([P, 2, ROT]), ALU.mult)
                V.drain()
                wait_b = ("ukv", 1, TT - 1)
                dve.wait_ge(free[bank(wait_b)], n_use(L, wait_b) + 1)
                for t in range(TT):
                    V.tensor_tensor(kb[:, t, :, NOPE:], kr[:, t:t + 1, :].broadcast_to([P, HEADS, ROT]),
                                    kt_tmp[:, t:t + 1, :].broadcast_to([P, HEADS, ROT]), ALU.add)
                q_tmp = rope_tmp[:, :, 0:HEADS * ROT].rearrange("p t (h d) -> p t h d", d=ROT)
                V.drain()
                for t in range(TT):
                    for f in range(2):
                        V.tensor_tensor(rot_view(q_tmp[:, t], f), rot_view(qb[:, t, :, NOPE:], 1 - f),
                                        rot_view(sin_b[:, t % 2:t % 2 + 1, :], f).broadcast_to([P, HEADS, 2, ROT // 4]),
                                        ALU.mult)
                V.drain()
                for t in range(TT):
                    V.tensor_tensor(qb[:, t, :, NOPE:], qb[:, t, :, NOPE:],
                                    cos_b[:, t % 2:t % 2 + 1, :].broadcast_to([P, HEADS, ROT]), ALU.mult)
                V.drain()
                V.tensor_tensor(qb[:, :, :, NOPE:], qb[:, :, :, NOPE:], q_tmp, ALU.add)
                V.drain()
                dve.sem_inc(b_ready, 1)
                for i in range(NU + 2):
                    if i < NU:
                        d = HD if UNITS[i][0] == "a" else QK_B
                        wait_full(dve, L, ("s", i))
                        V.tensor_reduce(out=mx[:, i, :], in_=ps[:, i % 2, :].rearrange("p (q k) -> p q k", q=2),
                                        op=ALU.max, axis=AX_X)
                        V.drain()
                        V.tensor_scalar(nmx[:, i, :], mx[:, i, :], -d ** -0.5, None, ALU.mult).then_inc(max_ready, 1)
                    if 0 <= i - 1 < NU:
                        u = i - 1
                        wait_full(dve, L, ("pt", u))
                        if u >= 2:
                            wait_full(dve, L, ("o", u - 2))
                        V.tensor_copy(prob_t[:, u % 2, :, :], ps[:, 2 + u % 2, :].rearrange("p (a b) -> p a b", a=2))
                        V.reciprocal(rin[:, u, :], sme[:, u, :])
                        V.drain()
                        dve.sem_inc(free[2 + u % 2], 1)
                        dve.sem_inc(pt_ready, 1)
                    if 0 <= i - 2 < NU:
                        u = i - 2
                        group, s, h, _ = UNITS[u]
                        b = bank(("o", u))
                        wait_full(dve, L, ("o", u))
                        col = h * HD + (512 if group == "b" else 0)
                        V.tensor_tensor(o_sb[:, 2 * s:2 * s + 2, col:col + HD],
                                        ps[:, b, 0:2 * HD].rearrange("p (q d) -> p q d", q=2),
                                        rin[:, u, :].rearrange("p (q o) -> p q o", o=1).broadcast_to([P, 2, HD]),
                                        ALU.mult).then_inc(free[b], 1)
                ada_finish(n0 + GATE_A)
                dve.wait_ge(o_root, L + 1)
                V.reciprocal(st_o[:, 0, :], st_o[:, 1, :])
                V.drain()
                for t in range(TT):
                    for g in range(2):
                        o = o_sb[:, t, 512 * g:512 * g + 512]
                        V.tensor_scalar(o, o, st_o[:, 0, 2 * t + g:2 * t + g + 1], None, ALU.mult)
                V.drain()
                dve.sem_inc(o_ready, 1)
                for k in range(KD):
                    dve.wait_ge(ot_hi_ready, KD * L + k + 1)
                    V.scalar_tensor_tensor(out=h_lo[:, k, :], in0=ps[:, k % 4, :],
                                           scalar=par[:, L, PC_GOUT + k:PC_GOUT + k + 1],
                                           in1=h_hi[:, k, :].bitcast(F32), op0=ALU.mult, op1=ALU.subtract)
                    V.drain()
                    dve.sem_inc(free[k % 4], 1)
                    dve.sem_inc(ot_ready, 1)
                V.memset(ssum[:], 0.0)
                V.drain()
                n_sq = KD + 2 * KD * L
                for m in range(KD):
                    if m % 4 == 0:
                        ada_start(n0 + SHIFT_F + m // 4)
                    for e in range(2):
                        ada_slot(n0 + SHIFT_F + m // 4, 2 * (m % 4) + e)
                    update_x(L, ("wo", m), m, GATE_A)
                    if m >= 1:
                        add_square(n_sq + m - 1)
                    if m == 4:
                        ada_finish(n0 + SHIFT_F)
                add_square(n_sq + KD - 1)
                dve.sem_inc(ssum_ready, 1)
                ada_finish(n0 + SCALE_F)
                normalise(L, 1)
                for g, n in enumerate(GROUPS):
                    first = sum(GROUPS[:g])
                    n_vec = n0 + GATE_F + g
                    ada = g == 0 or L + 1 < DEPTH
                    if ada:
                        ada_start(n_vec)

                    def tile(i, quad, ada_kt):
                        e = i % 2
                        at = 4 * quad + (first + i)
                        for half in range(2):
                            key = ("up", g, i, half)
                            b = bank(key)
                            dve.wait_ge(mid_tap, 8 * quad + (2 * (L * FT + first + i) + half + 1))
                            for tap, (dst, src) in ((0, (1, 0)), (2, (0, 1))):
                                u3 = u_sb[:, e, half, :].rearrange("p (s t) -> p s t", s=2)
                                p3 = ps[:, b, :].rearrange("p (s t) -> p s t", s=2)
                                V.scalar_tensor_tensor(
                                    out=u3[:, :, dst:dst + SEQ - 1], in0=p3[:, :, src:src + SEQ - 1],
                                    scalar=par[:, L, bass.ds(at + (PC_CW + tap * 2 * FT + half * FT), 1)],
                                    in1=u3[:, :, dst:dst + SEQ - 1], op0=ALU.mult, op1=ALU.add)
                                V.drain()
                            dve.sem_inc(free[b], 1)
                        dve.sem_inc(taps_done, 1)
                        if ada_kt is not None:
                            ada_slot(*ada_kt)
                        dve.wait_ge(sil_ready, 4 * quad + (L * FT + first + i + 1))
                        V.tensor_tensor(af[:, e, :], sil[:, e, :], u_sb[:, e, 0, :], ALU.mult)
                        V.drain()
                        dve.sem_inc(af_ready, 1)
                        dve.wait_ge(a_hi_ready, 4 * quad + (L * FT + first + i + 1))
                        lo_at = bass.ds(4 * quad + i, 1)
                        V.tensor_tensor(a_lo[:, lo_at, :], af[:, e:e + 1, :], a_hi[:, lo_at, :].bitcast(F32),
                                        ALU.subtract).then_inc(a_ready, 1)

                    for quad in range((n + 3) // 4):
                        for i in range(min(4, n - 4 * quad)):
                            tile(i, quad, (n_vec, 4 * quad + i) if ada else None)
                    if ada:
                        for kt in range(n, KD):
                            ada_slot(n_vec, kt)
                        ada_finish(n_vec)
                    if g == len(GROUPS) - 1:
                        V.memset(ssum[:], 0.0)
                        V.drain()
                    n_sq = 2 * KD + 2 * KD * L
                    for m in range(KD):
                        update_x(L, ("down", g, m), m, GATE_F, done=g == len(GROUPS) - 1)
                        if g == len(GROUPS) - 1 and m >= 1:
                            add_square(n_sq + m - 1)
                add_square(n_sq + KD - 1)
                dve.sem_inc(ssum_ready, 1)
            dve.wait_ge(root_ready, 2 * DEPTH + 1)
            V.reciprocal(rstd[:], root[:])
            V.drain()
            for k in range(KD):
                V.scalar_tensor_tensor(out=x[:, k, :], in0=x[:, k, :], scalar=gfin[:, k:k + 1], in1=rstd[:],
                                       op0=ALU.mult, op1=ALU.mult).then_inc(y_done, 1)


_BLOCKS = [u for u in range(NU) if UNITS[u][3]]


def _block_of(u):
    return max(n for n, first in enumerate(_BLOCKS) if first <= u)


def QT_BUF(u):
    return _block_of(u) % 2


def QT_DONE(L, u):
    return L * len(_BLOCKS) + _block_of(u) + 1


def QT_LAST_READER(u):
    n = _block_of(u)
    return _BLOCKS[n - 1] - 1 if n >= 2 else None


def _tables():
    out = []
    for d in (HD, ROT):
        q = d // 4
        t = np.arange(SEQ)
        pos = np.stack([t // GRID_W, t % GRID_W], -1).astype(np.float32)
        inv = np.float32(THETA) ** (-np.arange(q, dtype=np.float32) / np.float32(q))
        ang = (pos[:, :, None] * inv).astype(np.float32)
        c, s = np.cos(ang), np.sin(ang)
        cos = np.stack([c, c], 2).reshape(2, P, d).transpose(1, 0, 2).reshape(P, 2 * d)
        sin = np.stack([-s, s], 2).reshape(2, P, d).transpose(1, 0, 2).reshape(P, 2 * d)
        out.append(np.stack([cos, sin], 1))
    return np.ascontiguousarray(np.concatenate(out, -1), np.float32)


def _columns(v, n):
    return np.moveaxis(v.reshape(*v.shape[:-1], n, P), -1, 0)


def _pack(inp):
    f = {k: np.asarray(v) for k, v in inp.items()}
    xs = np.concatenate([f["x_prompt"].reshape(SEQ, D_MODEL), f["x_sample"].reshape(SEQ, D_MODEL)], 0)
    x_t = xs.T.reshape(KD, P, T).transpose(1, 0, 2)
    cs = np.concatenate([f["c_prompt"], f["c_sample"]], 0)
    c_t = cs.reshape(NSEQ, KD, P).transpose(2, 1, 0)
    ada = f["w_ada"].reshape(DEPTH, KD, P, N_MOD, SLOT).transpose(0, 3, 1, 2, 4).reshape(DEPTH * N_MOD * KD, P, SLOT)
    slots = np.zeros((DEPTH, SLOTS, P, SLOT), np.float32)
    w_in = f["w_in"]
    wa, kva = HEADS * HD, KV_HEADS * HD
    order = []
    base_cq = wa + 2 * kva
    order += list(range(base_cq, base_cq + Q_LORA + KV_LORA + ROT))
    for p in range(4):
        for g in range(2):
            order += list(range((p + 4 * g) * HD, (p + 4 * g + 1) * HD))
    order += list(range(wa, wa + 2 * kva))
    w_in = w_in[:, :, order]
    for c, (col, width) in enumerate(CHUNKS):
        v = w_in[:, :, col:col + width].reshape(DEPTH, 2, 4, P, width).transpose(0, 1, 3, 2, 4)
        slots[:, S_IN + 2 * c:S_IN + 2 * c + 2, :, 0:4 * width] = v.reshape(DEPTH, 2, P, 4 * width)
    width = 2 * QK_B
    v = f["w_uq"].reshape(DEPTH, 2, P, 4, width).transpose(0, 3, 2, 1, 4)
    slots[:, S_UQ:S_UQ + 4, :, 0:2 * width] = v.reshape(DEPTH, 4, P, 2 * width)
    v = f["w_ukv"].reshape(DEPTH, P, HEADS, 2, HD).transpose(0, 3, 1, 2, 4)
    slots[:, S_UKV:S_UKV + 2, :, 0:HEADS * HD] = v.reshape(DEPTH, 2, P, HEADS * HD)

    def by_column_tile(w, k):
        n = w.shape[2] // P
        return w.reshape(DEPTH, k, P, n, P).transpose(0, 3, 2, 1, 4).reshape(DEPTH, n, P, k * P)

    slots[:, S_WO:S_WO + KD] = by_column_tile(f["w_o"], KD)
    up = by_column_tile(f["w_up"], KD)
    first = 0
    for g, n in enumerate(GROUPS):
        s = S_UP[g]
        slots[:, s:s + 2 * n:2] = up[:, first:first + n]
        slots[:, s + 1:s + 2 * n:2] = up[:, FT + first:FT + first + n]
        s = S_DOWN[g]
        slots[:, s:s + KD, :, 0:n * P] = by_column_tile(f["w_down"][:, first * P:(first + n) * P], n)
        first += n
    par = [_columns(f["g_attn"], KD), _columns(f["g_ffn"], KD),
           _columns(f["g_out_a"], KD // 2), _columns(f["g_out_b"], KD // 2),
           _columns(f["g_cq"], 2), _columns(f["g_ckv"], 1), _columns(f["b_ada"], N_MOD * KD),
           _columns(f["conv_w"], 2 * FT).reshape(P, DEPTH, 6 * FT), _columns(f["conv_b"], 2 * FT)]
    gqk = np.stack([f["g_q_a"], f["g_k_a"]], 1)
    ins = {
        "x_t": x_t, "c_t": c_t, "w_slots": slots.reshape(DEPTH * SLOTS, P, SLOT), "ada_slots": ada,
        "params": np.concatenate(par, -1), "g_qk": np.broadcast_to(gqk, (P, *gqk.shape)),
        "g_fin": _columns(f["g_final"], KD), "tables": _tables(), "ident": np.eye(P, dtype=np.float32),
    }
    return {k: np.ascontiguousarray(v) for k, v in ins.items()}


def kernel(**inputs):
    import concourse.bacc as bacc
    from concourse.bass_utils import run_bass_kernel_spmd

    arrays = _pack(inputs)
    nc = bacc.Bacc("TRN2", target_bir_lowering=False, num_devices=1)
    args = [nc.dram_tensor(k, v.shape, F32, kind="ExternalInput").ap() for k, v in arrays.items()]
    y = nc.dram_tensor("y_t", (P, KD, T), F32, kind="ExternalOutput").ap()
    encoder_kernel(nc, *args, y)
    r = run_bass_kernel_spmd(nc, [arrays], core_ids=[0])
    y = np.asarray(r.results[0]["y_t"]).transpose(2, 1, 0).reshape(NSEQ, SEQ, D_MODEL)
    return y[0:1], y[1:2]
```

```python
from contextlib import ExitStack

import concourse.bass as bass
import numpy as np
from concourse import mybir

F32 = mybir.dt.float32
F32R = mybir.dt.float32r
ALU = mybir.AluOpType
ACT = mybir.ActivationFunctionType
AX_X = mybir.AxisListType.X

P = 128
D_MODEL = 1024
DEPTH = 2
SEQ = 256
NSEQ = 2
T = NSEQ * SEQ
TT = T // P
KD = D_MODEL // P
GRID_W = 64
THETA = 10000.0
EPS = 1e-6
HEADS = 8
HD = 64
KV_HEADS = 2
NOPE = 64
ROT = 32
QK_B = NOPE + ROT
Q_LORA = 256
KV_LORA = 128
D_FF = 2816
FT = D_FF // P
N_MOD = 6

C_CQ = 0
C_CKV = C_CQ + Q_LORA
C_KR = C_CKV + KV_LORA
C_Q = C_KR + ROT
C_K = C_Q + HEADS * HD
C_V = C_K + KV_HEADS * HD
D_IN = C_V + KV_HEADS * HD
CHUNKS = [(C_CQ, 256), (C_CKV, 160), (C_Q, 256), (C_Q + 256, 256), (C_K, 256)]

SLOT = 1024
RING = 4
GROUPS = [8, 8, 6]
S_IN = 0
S_UQ = S_IN + 2 * len(CHUNKS)
S_UKV = S_UQ + 4
S_WO = S_UKV + 2
S_FFN = S_WO + KD
S_UP, S_DOWN = [], []
_at = S_FFN
for _n in GROUPS:
    S_UP.append(_at)
    S_DOWN.append(_at + 2 * _n)
    _at += 2 * _n + KD
SLOTS = _at
ROUNDS = SLOTS // RING
assert SLOTS % RING == 0 and sum(GROUPS) == FT

PC_GATTN = 0
PC_GFFN = PC_GATTN + KD
PC_GOUT = PC_GFFN + KD
PC_GCQ = PC_GOUT + KD
PC_GCKV = PC_GCQ + 2
PC_BADA = PC_GCKV + 1
PC_CW = PC_BADA + N_MOD * KD
PC_CB = PC_CW + 3 * 2 * FT
NPC = PC_CB + 2 * FT
SHIFT_A, SCALE_A, GATE_A, SHIFT_F, SCALE_F, GATE_F = range(N_MOD)

UNITS = [("a", s, p + 4 * g, g == 0) for s in range(NSEQ) for p in range(4) for g in range(2)]
UNITS += [("b", s, h, True) for s in range(NSEQ) for h in range(HEADS)]
NU = len(UNITS)
MOD_AT_UNIT = 15
QK_BLOCKS = [(0, 0, 4), (0, 4, 4), (1, 8, 2)]


MOD_AFTER_WO = {2: SHIFT_F, 7: SCALE_F}
ADA_AT_WO = {0: [(SHIFT_F, 4), (SHIFT_F, 5)], 1: [(SHIFT_F, 6), (SHIFT_F, 7)], 3: [(SCALE_F, 0), (SCALE_F, 1)],
             4: [(SCALE_F, 2), (SCALE_F, 3)], 5: [(SCALE_F, 4), (SCALE_F, 5)], 6: [(SCALE_F, 6)], 7: [(SCALE_F, 7)]}
ADA_AT_UNIT = {4: (GATE_A, 6), 8: (GATE_A, 7), 19: (SHIFT_F, 0), 22: (SHIFT_F, 1), 25: (SHIFT_F, 2), 28: (SHIFT_F, 3)}
STATS_AT_UNIT = {11: (0, 0), 19: (0, 1), 27: (1, 0)}


def plan_banks():
    count, use = [0] * 8, {}

    def take(key, bank):
        use[key] = (bank, count[bank])
        count[bank] += 1

    take("norm1", 6)
    for c in range(len(CHUNKS)):
        for t in range(TT):
            take(("proj", c, t), t)
    for j in range(3):
        take(("lat", j), 4 + j)
    for s in range(4):
        for t in range(TT):
            take(("uq", s, t), t)
    for s in range(2):
        for t in range(TT):
            take(("ukv", s, t), t)
    take("kat", 7)
    pairs = 0
    for i in range(-1, NU + 2):
        if i + 1 < NU and UNITS[i + 1][3]:
            take(("qt", i + 1), 4 + pairs % 2)
            pairs += 1
        if 0 <= i < NU:
            take(("s", i), i % 2)
        if 0 <= i - 1 < NU:
            take(("pt", i - 1), 2 + (i - 1) % 2)
        if 0 <= i - 2 < NU:
            take(("o", i - 2), 6 + i % 2)
        if i == MOD_AT_UNIT:
            take(("mod", GATE_A), 7)
    for k in range(KD):
        take(("ot", k), k % 4)
    for m in range(KD):
        take(("wo", m), 4 + m % 2)
        if m in MOD_AFTER_WO:
            take(("mod", MOD_AFTER_WO[m]), 7)
    take("norm2", 6)
    for g, n in enumerate(GROUPS):
        for i in range(n):
            take(("up", g, i, 0), 2 * (i % 2))
            take(("up", g, i, 1), 2 * (i % 2) + 1)
        take(("mod", (GATE_F + g) % N_MOD), 7)
        for m in range(KD):
            take(("down", g, m), 4 + m % 2)
    return use, count


USE, USES = plan_banks()
BEFORE = {7: 2, 0: 1, 1: 1}

ADA_AFTER = {1: 4, 2: 2, 3: 2, 4: 8, 5: 4, 6: 4, 7: 4, 8: 2, 9: 2}
ADA_NEXT = {11: 4, 13: 2, 14: 2, 17: 4, 19: 2, 20: 2}


def encoder_kernel(nc, x_t, c_t, w_slots, ada_slots, params, g_qk, g_fin, tables, ident_d, y_t):
    ctx = ExitStack()
    with ctx:
        base = [16512]

        def sem(name):
            return ctx.enter_context(nc.semaphore(name))

        def put(name, shape, dt=F32, at=None):
            size = 4 * int(np.prod(shape[1:]))
            if at is None:
                at = base[0]
                base[0] += (size + 31) // 32 * 32
            return nc.alloc_sbuf_tensor_at(name, shape, dt, offset=at)

        x = put("x", [P, KD, T])
        at_h = base[0]
        h_hi = put("h_hi", [P, KD, T], F32R)
        h_lo = put("h_lo", [P, KD, T], F32R)
        at_act = base[0]
        a_hi = put("a_hi", [P, 8, T], F32R)
        a_lo = put("a_lo", [P, 8, T], F32R)
        w_raw = put("w_raw", [P, RING, SLOT])
        w_hi = put("w_hi", [P, RING, SLOT], F32R)
        w_lo = put("w_lo", [P, RING, SLOT], F32R)
        ada_raw = put("ada_raw", [P, 4, SLOT])
        ada_acc = put("ada_acc", [P, NSEQ, SLOT])
        at_proj = base[0]
        proj = put("proj", [P, TT, D_IN])
        at_o = base[0]
        o_sb = put("o_sb", [P, TT, D_MODEL])
        rstd = put("rstd", [P, T])
        ssum = put("ssum", [P, T])
        mod = put("mod", [P, N_MOD, KD, NSEQ])
        cact = put("cact", [P, KD, NSEQ])
        par = put("par", [P, DEPTH, NPC])
        gqk = put("gqk", [P, DEPTH, 2, HD])
        gfin = put("gfin", [P, KD])
        tab = put("tab", [P, 2, 2 * (HD + ROT)])
        ident = put("ident", [P, P])
        ones = put("ones", [P, P])
        eps = put("eps", [P, 1])
        kr_tmp = put("kr_tmp", [P, TT, ROT])
        kr_rot = put("kr_rot", [P, TT, ROT])
        shift_row = put("shift_row", [NSEQ, SLOT])
        cg = put("cg", [P, 2, 2, HD])
        sg_t = put("sg_t", [P, 2, 2, HD])
        st_lat = put("st_lat", [P, 2, 8])
        st_qk = put("st_qk", [P, 2, 40])
        st_o = put("st_o", [P, 2, 8])
        mx = put("mx", [P, NU, 2])
        nmx = put("nmx", [P, NU, 2])
        sme = put("sme", [P, NU, 2])
        rin = put("rin", [P, NU, 2])
        assert base[0] <= nc.sbuf_usable_end, base[0]
        qb = put("qb", [P, TT, HEADS, QK_B], at=at_h)
        shift0 = put("shift0", [P, KD, SLOT], at=at_h)
        kb = put("kb", [P, TT, HEADS, QK_B], at=at_h + 12288)
        vb = put("vb", [P, TT, HEADS * HD], at=at_h + 24576)
        ct_hi = put("ct_hi", [P, 3, T], F32R, at=at_act)
        ct_lo = put("ct_lo", [P, 3, T], F32R, at=at_act + 6144)
        prob = put("prob", [P, 2, 2, SEQ], at=at_act + 12288)
        prob_t = put("prob_t", [P, 2, 2, SEQ], at=at_act + 16384)
        qk_t = put("qk_t", [P, 2, T], at=at_act + 20480)
        ka_t = put("ka_t", [P, T], at=at_act + 24576)
        qb_tmp = put("qb_tmp", [P, TT, HEADS, ROT], at=at_act + 26624)
        junk_o = put("junk_o", [P, 512], at=at_act)
        xn = put("xn", [P, 2, T], at=at_o)
        hf = put("hf", [P, 2, T], at=at_o + 4096)
        root = put("root", [P, T], at=at_o + 8192)
        sq_x = put("sq_x", [P, 2, T], at=at_o + 10240)
        sq_qk = put("sq_qk", [P, TT, 4 * HD], at=at_o)
        rope_tmp = put("rope_tmp", [P, TT, 4 * HD], at=at_o + 4096)
        junk = put("junk", [P, 512], at=at_o + 14336)
        u_sb = put("u_sb", [P, 2, 2, T], at=at_proj)
        sil = put("sil", [P, 2, T], at=at_proj + 8192)
        af = put("af", [P, 2, T], at=at_proj + 12288)
        ps = ctx.enter_context(nc.psum_tensor("ps", [P, 8, 512], F32))

        def qk_stat(r, h0, nh):
            return st_qk[:, r, :].rearrange("p (t h) -> p t h", t=TT)[:, :, h0:h0 + nh]

        cos_a = tab[:, 0, 0:2 * HD].rearrange("p (e d) -> p e d", e=2)
        sin_a = tab[:, 1, 0:2 * HD].rearrange("p (e d) -> p e d", e=2)
        cos_b = tab[:, 0, 2 * HD:].rearrange("p (e d) -> p e d", e=2)
        sin_b = tab[:, 1, 2 * HD:].rearrange("p (e d) -> p e d", e=2)

        c_landed = sem("c_landed")
        shift0_landed = [sem(f"shift0_landed{k}") for k in range(2)]
        row_ready = sem("row_ready")
        loaded = sem("loaded")
        raw_landed = [sem(f"raw_landed{j}") for j in range(RING)]
        raw_free = sem("raw_free")
        hi_done = sem("hi_done")
        split_done = sem("split_done")
        slot_free = sem("slot_free")
        ada_landed = [sem(f"ada_landed{j}") for j in range(4)]
        ada_used = sem("ada_used")
        acc_ready = sem("acc_ready")
        mod_ready = sem("mod_ready")
        c_ready = sem("c_ready")
        full = [sem(f"bank_full{b}") for b in range(8)]
        free = [sem(f"bank_free{b}") for b in range(8)]
        const_ready = sem("const_ready")
        ssum_ready = sem("ssum_ready")
        root_ready = sem("root_ready")
        xn_ready = sem("xn_ready")
        h_hi_ready = sem("h_hi_ready")
        h_ready = sem("h_ready")
        sq_q = sem("sq_q")
        lat_sq = sem("lat_sq")
        lat_ready = sem("lat_ready")
        ct_hi_ready = sem("ct_hi_ready")
        ct_ready = sem("ct_ready")
        qk_sq = sem("qk_sq")
        qk_ms = sem("qk_ms")
        qk_root = sem("qk_root")
        qk_ready = sem("qk_ready")
        kr_ready = sem("kr_ready")
        ka_ready = sem("ka_ready")
        b_ready = sem("b_ready")
        qt_ready = sem("qt_ready")
        max_ready = sem("max_ready")
        exp_ready = sem("exp_ready")
        pt_ready = sem("pt_ready")
        o_root = sem("o_root")
        o_ready = sem("o_ready")
        ot_hi_ready = sem("ot_hi_ready")
        ot_ready = sem("ot_ready")
        x_upd = sem("x_upd")
        sq_ready = sem("sq_ready")
        mid_tap = sem("mid_tap")
        taps_done = sem("taps_done")
        sil_ready = sem("sil_ready")
        af_ready = sem("af_ready")
        a_hi_ready = sem("a_hi_ready")
        a_ready = sem("a_ready")
        y_done = sem("y_done")
        stored = sem("stored")

        def bank(key):
            return USE[key][0]

        def n_use(L, key):
            b, n = USE[key]
            return L * USES[b] + n + BEFORE.get(b, 0)

        def wait_full(eng, L, key, plus=0):
            eng.wait_ge(full[bank(key)], n_use(L, key) + 1 + plus)

        def wait_free(eng, L, key, plus=0):
            n = n_use(L, key) + plus
            if type(n) is not int or n > 0:
                eng.wait_ge(free[bank(key)], n)

        def rot_view(ap, f):
            return ap.rearrange("p t (s f d) -> p t s f d", s=2, f=2)[:, :, :, f, :]

        block = ctx.enter_context(nc.Block())

        N_LOADS = 7

        @block.sync
        def _(sp):
            def load_ada(n_vec, kt):
                sp.wait_ge(ada_used, 8 * n_vec + kt + 1)
                sp.dma_start(ada_raw[:, kt % 4, :], ada_slots[8 * n_vec + kt]).then_inc(ada_landed[kt % 4], 16)

            def load_round(L, r):
                for j in range(RING):
                    sp.wait_ge(raw_free, L * SLOTS + RING * r + j + 1)
                    sp.dma_start(w_raw[:, j, :], w_slots[L * SLOTS + RING * r + j]).then_inc(raw_landed[j], 16)

            sp.dma_start(cact[:], c_t).then_inc(c_landed, 16)
            for half in range(2):
                for kt in range(2):
                    load_ada(0, 4 * half + kt)
                sp.dma_start(shift0[:, 4 * half:4 * half + 4, :],
                             ada_slots[SHIFT0 + 4 * half:SHIFT0 + 4 * half + 4].rearrange("k p n -> p k n")
                             ).then_inc(shift0_landed[half], 16)
                for kt in range(2, 4):
                    load_ada(0, 4 * half + kt)
                sp.dma_start(x[:, 4 * half:4 * half + 4, :], x_t[:, 4 * half:4 * half + 4, :]).then_inc(loaded, 16)
            sp.dma_start(par[:], params).then_inc(loaded, 16)
            sp.dma_start(gqk[:], g_qk).then_inc(loaded, 16)
            sp.dma_start(gfin[:], g_fin).then_inc(loaded, 16)
            sp.dma_start(tab[:], tables).then_inc(loaded, 16)
            sp.dma_start(ident[:], ident_d).then_inc(loaded, 16)
            for L in range(DEPTH):
                a = [8 * (N_MOD * L + GATE_A - 1)]
                for r in range(ROUNDS):
                    load_round(L, r)
                    n = ADA_AFTER.get(r, 0) + (ADA_NEXT.get(r, 0) if L + 1 < DEPTH else 0)
                    for _ in range(n):
                        load_ada(a[0] // 8, a[0] % 8)
                        a[0] += 1
            for k in range(KD):
                sp.wait_ge(y_done, k + 1)
                sp.dma_start(y_t[:, k, :], x[:, k, :]).then_inc(stored, 16)
            sp.wait_ge(stored, 16 * KD)

        @block.gpsimd
        def _(pool):
            nc.gpsimd.memset(ones[:], 1.0)
            nc.gpsimd.memset(eps[:], EPS)
            nc.gpsimd.drain()
            pool.sem_inc(const_ready, 1)
            pool.sem_inc(raw_free, RING)

            def lo_slot(j, n):
                pool.wait_ge(hi_done, n + 1)
                nc.gpsimd.tensor_tensor(w_lo[:, j, :], w_raw[:, j, :], w_hi[:, j, :].bitcast(F32), ALU.subtract)
                nc.gpsimd.drain()
                pool.sem_inc(raw_free, 1)
                pool.sem_inc(split_done, 1)

            def lo_rounds(L, r0, r1):
                with pool.Fori(0, r1 - r0) as r:
                    for j in range(RING):
                        lo_slot(j, RING * r + (L * SLOTS + RING * r0 + j))

            for L in range(DEPTH):
                lo_rounds(L, 0, S_WO // RING)
                for s in range(S_WO, S_WO + 3):
                    lo_slot(s % RING, L * SLOTS + s)
                pool.wait_ge(kr_ready, L + 1)
                wait_b = ("uq", 3, TT - 1)
                pool.wait_ge(free[bank(wait_b)], n_use(L, wait_b) + 1)
                for t in range(TT):
                    for f in range(2):
                        nc.gpsimd.tensor_tensor(rot_view(qb_tmp[:, t], f), rot_view(qb[:, t, :, NOPE:], 1 - f),
                                                rot_view(sin_b[:, t % 2:t % 2 + 1, :], f).broadcast_to(
                                                    [P, HEADS, 2, ROT // 4]), ALU.mult)
                nc.gpsimd.drain()
                for t in range(TT):
                    nc.gpsimd.tensor_tensor(qb[:, t, :, NOPE:], qb[:, t, :, NOPE:],
                                            cos_b[:, t % 2:t % 2 + 1, :].broadcast_to([P, HEADS, ROT]), ALU.mult)
                    nc.gpsimd.tensor_copy(kb[:, t, :, NOPE:], kr_rot[:, t:t + 1, :].broadcast_to([P, HEADS, ROT]))
                nc.gpsimd.drain()
                nc.gpsimd.tensor_tensor(qb[:, :, :, NOPE:], qb[:, :, :, NOPE:], qb_tmp[:], ALU.add)
                nc.gpsimd.drain()
                pool.sem_inc(b_ready, 1)
                lo_slot((S_WO + 3) % RING, L * SLOTS + S_WO + 3)
                lo_rounds(L, S_WO // RING + 1, ROUNDS)

        @block.tensor
        def _(pe):
            mm = nc.tensor.matmul
            pe.sem_inc(slot_free, RING - 1)

            def slot(L, s):
                pe.wait_ge(split_done, L * SLOTS + s + 1)
                return s % RING

            def product(out, stat, mov, first, last, release=0):
                hh = mm(out, stat[0], mov[0], start=first, stop=False)
                hl = mm(out, stat[0], mov[1], start=False, stop=False)
                if release >= 1:
                    hh.then_inc(slot_free, 1)
                if release >= 2:
                    hl.then_inc(slot_free, 1)
                return mm(out, stat[1], mov[0], start=False, stop=last)

            def sum_mod(L, v, n_vec):
                pe.wait_ge(acc_ready, n_vec)
                b = 7
                if L is None:
                    pe.wait_ge(free[7], 1)
                else:
                    wait_free(pe, L, ("mod", v))
                for j in range(KD):
                    for s in range(NSEQ):
                        last = mm(ps[:, b, 2 * j + s:2 * j + s + 1], ada_acc[:, s, P * j:P * j + P], ones[:, 0:1],
                                  start=True, stop=True)
                last.then_inc(full[b], 1)

            def norm_sum(L, which, n):
                pe.wait_ge(ssum_ready, n + 1)
                wait_free(pe, L, which)
                mm(ps[:, 6, :], ones[:], ssum[:], start=True, stop=True).then_inc(full[6], 1)

            pe.wait_ge(const_ready, 1)
            pe.wait_ge(c_ready, 1)
            for k in range(KD):
                if k % 4 == 0:
                    pe.wait_ge(shift0_landed[k // 4], 16)
                for b in range(2):
                    last = mm(ps[0:NSEQ, b, :], cact[:, k, :], shift0[:, k, b * 512:(b + 1) * 512], start=(k == 0),
                              stop=(k == KD - 1))
                    if k == KD - 1:
                        last.then_inc(full[b], 1)
            pe.wait_ge(loaded, 16 * N_LOADS)
            pe.wait_ge(row_ready, 1)
            for j in range(KD):
                last = nc.tensor.transpose(ps[:, 7, 2 * j:2 * j + 2], shift_row[:, j * P:(j + 1) * P],
                                           ident[0:NSEQ, 0:NSEQ])
            last.then_inc(full[7], 1)
            sum_mod(None, SCALE_A, 1)

            for L in range(DEPTH):
                norm_sum(L, "norm1", 2 * L)
                for c, (col, width) in enumerate(CHUNKS):
                    halves = [0, 0]

                    def part(k, t, first, last, release=0):
                        j = halves[k // 4]
                        w = [r[:, j, (k % 4) * width:(k % 4 + 1) * width] for r in (w_hi, w_lo)]
                        st = [r[:, k, t * P:t * P + P] for r in (h_hi, h_lo)]
                        return product(ps[:, t, 0:width], st, w, first, last, release)

                    if c == 0:
                        for k in range(KD):
                            if k % 4 == 0:
                                halves[k // 4] = slot(L, S_IN + k // 4)
                            pe.wait_ge(h_ready, 16 * L + k + 1)
                            for t in range(TT):
                                if k == 0:
                                    wait_free(pe, L, ("proj", c, t))
                                last = part(k, t, k == 0, k == KD - 1, int(k == 0 and t == 0))
                                if k == KD - 1:
                                    last.then_inc(full[t], 1)
                    else:
                        for t in range(TT):
                            wait_free(pe, L, ("proj", c, t))
                            for k in range(KD):
                                if t == 0 and k % 4 == 0:
                                    halves[k // 4] = slot(L, S_IN + 2 * c + k // 4)
                                last = part(k, t, k == 0, k == KD - 1, 2 * int(k == 0 and t == 0))
                            last.then_inc(full[t], 1)
                pe.wait_ge(lat_ready, L + 1)
                for j in range(3):
                    wait_free(pe, L, ("lat", j))
                    for t in range(TT):
                        last = nc.tensor.transpose(ps[:, 4 + j, t * P:t * P + P], proj[:, t, j * P:j * P + P], ident[:])
                    last.then_inc(full[4 + j], 1)
                width = 2 * QK_B
                for s in range(4):
                    j = slot(L, S_UQ + s)
                    if s == 0:
                        pe.wait_ge(ct_ready, 3 * L + 2)
                    for t in range(TT):
                        wait_free(pe, L, ("uq", s, t))
                        for k in range(2):
                            last = product(ps[:, t, 0:width], [r[:, k, t * P:t * P + P] for r in (ct_hi, ct_lo)],
                                           [r[:, j, k * width:(k + 1) * width] for r in (w_hi, w_lo)], k == 0, k == 1,
                                           (1 + int(s == 0)) * int(k == 0 and t == 0))
                        last.then_inc(full[t], 1)
                pe.wait_ge(ct_ready, 3 * L + 3)
                for s in range(2):
                    j = slot(L, S_UKV + s)
                    for t in range(TT):
                        wait_free(pe, L, ("ukv", s, t))
                        product(ps[:, t, :], [r[:, 2, t * P:t * P + P] for r in (ct_hi, ct_lo)],
                                [r[:, j, 0:512] for r in (w_hi, w_lo)], True, True, int(t == 0)).then_inc(full[t], 1)
                pe.wait_ge(qk_ready, len(QK_BLOCKS) * (L + 1))
                wait_free(pe, L, "kat")
                for t in range(TT):
                    last = nc.tensor.transpose(ps[:, 7, t * P:t * P + P], proj[:, t, C_K:C_K + P], ident[:])
                last.then_inc(full[7], 1)
                for i in range(-1, NU + 2):
                    if i + 1 < NU and UNITS[i + 1][3]:
                        group, s, h, _ = UNITS[i + 1]
                        b = bank(("qt", i + 1))
                        wait_free(pe, L, ("qt", i + 1))
                        if group == "b" and UNITS[i][0] == "a":
                            pe.wait_ge(b_ready, L + 1)
                        for q in range(2):
                            if group == "a":
                                last = nc.tensor.transpose(ps[:, b, q * P:q * P + P],
                                                           proj[:, 2 * s + q, C_Q + h * P:C_Q + h * P + P], ident[:])
                            else:
                                nc.tensor.transpose(ps[0:QK_B, b, q * P:q * P + P], qb[:, 2 * s + q, h, :], ident[:])
                                last = nc.tensor.transpose(ps[0:QK_B, b, SEQ + q * P:SEQ + q * P + P],
                                                           kb[:, 2 * s + q, h, :], ident[:])
                        last.then_inc(full[b], 1)
                    if 0 <= i < NU:
                        group, s, h, _ = UNITS[i]
                        wait_free(pe, L, ("s", i))
                        pe.wait_ge(qt_ready, QT_DONE(L, i))
                        if i == 0:
                            pe.wait_ge(ka_ready, L + 1)
                        buf = QT_BUF(i)
                        for q in range(2):
                            if group == "a":
                                o = 64 * (h // 4)
                                st, mv = qk_t[o:o + 64, buf, q * P:q * P + P], ka_t[o:o + 64, s * SEQ:(s + 1) * SEQ]
                            else:
                                st, mv = qk_t[0:QK_B, buf, q * P:q * P + P], qk_t[0:QK_B, buf, SEQ:2 * SEQ]
                            last = mm(ps[:, i % 2, q * SEQ:(q + 1) * SEQ], st, mv, start=True, stop=True)
                        last.then_inc(full[i % 2], 1)
                    if 0 <= i - 1 < NU:
                        u = i - 1
                        wait_free(pe, L, ("pt", u))
                        pe.wait_ge(exp_ready, L * NU + u + 1)
                        for q in range(2):
                            for k in range(2):
                                last = nc.tensor.transpose(
                                    ps[:, 2 + u % 2, k * SEQ + q * P:k * SEQ + q * P + P],
                                    prob[:, u % 2, q, k * P:k * P + P], ident[:])
                        last.then_inc(full[2 + u % 2], 1)
                    if 0 <= i - 2 < NU:
                        u = i - 2
                        group, s, h, _ = UNITS[u]
                        b = bank(("o", u))
                        wait_free(pe, L, ("o", u))
                        pe.wait_ge(pt_ready, L * NU + u + 1)
                        for q in range(2):
                            for k in range(2):
                                if group == "a":
                                    v = proj[:, 2 * s + k, C_V + HD * (h // 4):C_V + HD * (h // 4) + HD]
                                else:
                                    v = vb[:, 2 * s + k, h * HD:(h + 1) * HD]
                                last = mm(ps[:, b, q * HD:(q + 1) * HD], prob_t[:, u % 2, k, q * P:q * P + P], v,
                                          start=(k == 0), stop=(k == 1))
                        last.then_inc(full[b], 1)
                    if i == MOD_AT_UNIT:
                        sum_mod(L, GATE_A, N_MOD * L + GATE_A)
                for k in range(KD):
                    if k % 4 == 0:
                        pe.wait_ge(o_ready, 2 * L + k // 4 + 1)
                    wait_free(pe, L, ("ot", k))
                    for t in range(TT):
                        last = nc.tensor.transpose(ps[:, k % 4, t * P:t * P + P], o_sb[:, t, k * P:k * P + P], ident[:])
                    last.then_inc(full[k % 4], 1)
                for m in range(KD):
                    j = slot(L, S_WO + m)
                    wait_free(pe, L, ("wo", m))
                    for k in range(KD):
                        if m == 0:
                            pe.wait_ge(ot_ready, KD * L + k + 1)
                        last = product(ps[:, 4 + m % 2, :], [r[:, j, k * P:k * P + P] for r in (w_hi, w_lo)],
                                       [r[:, k, :] for r in (h_hi, h_lo)], k == 0, k == KD - 1, int(k == 0))
                    last.then_inc(full[4 + m % 2], 1)
                    if m in MOD_AFTER_WO:
                        sum_mod(L, MOD_AFTER_WO[m], N_MOD * L + MOD_AFTER_WO[m])
                norm_sum(L, "norm2", 2 * L + 1)
                for g, n in enumerate(GROUPS):
                    peeled = 0
                    if g == 0:
                        peeled = 1
                        for k in range(KD):
                            pe.wait_ge(h_ready, 16 * L + 8 + k + 1)
                            for j in range(RING):
                                key = ("up", 0, j // 2, j % 2)
                                if k == 0:
                                    slot(L, S_UP[0] + j)
                                    wait_free(pe, L, key)
                                last = product(ps[:, bank(key), :], [r[:, j, k * P:k * P + P] for r in (w_hi, w_lo)],
                                               [r[:, k, :] for r in (h_hi, h_lo)], k == 0, k == KD - 1,
                                               int((k == 0 and j == 0) or (k == KD - 1 and j > 0)))
                                if k == KD - 1:
                                    last.then_inc(full[bank(key)], 1)
                    with pe.Fori(peeled, n // 2) as it:
                        for e in range(2):
                            for half in range(2):
                                key = ("up", g, e, half)
                                pe.wait_ge(split_done, 4 * it + (L * SLOTS + S_UP[g] + 2 * e + half + 1))
                                wait_free(pe, L, key, it)
                                j = (S_UP[g] + 2 * e + half) % RING
                                for k in range(KD):
                                    last = product(ps[:, bank(key), :],
                                                   [r[:, j, k * P:k * P + P] for r in (w_hi, w_lo)],
                                                   [r[:, k, :] for r in (h_hi, h_lo)], k == 0, k == KD - 1, int(k == 0))
                                last.then_inc(full[bank(key)], 1)
                    v = (GATE_F + g) % N_MOD
                    if g == 0 or L + 1 < DEPTH:
                        sum_mod(L, v, N_MOD * L + GATE_F + g)
                    with pe.Fori(0, KD // 4) as it:
                        for e in range(4):
                            key = ("down", g, e)
                            pe.wait_ge(split_done, 4 * it + (L * SLOTS + S_DOWN[g] + e + 1))
                            wait_free(pe, L, key, 2 * it)
                            j = (S_DOWN[g] + e) % RING
                            for k in range(n):
                                if e == 0:
                                    pe.wait_ge(a_ready, L * FT + sum(GROUPS[:g]) + k + 1)
                                last = product(ps[:, bank(key), :],
                                               [r[:, j, k * P:k * P + P] for r in (w_hi, w_lo)],
                                               [r[:, k, :] for r in (a_hi, a_lo)], k == 0, k == n - 1, int(k == 0))
                            last.then_inc(full[bank(key)], 1)
            pe.wait_ge(ssum_ready, 2 * DEPTH + 1)
            pe.wait_ge(free[6], DEPTH * USES[6])
            mm(ps[:, 6, :], ones[:], ssum[:], start=True, stop=True).then_inc(full[6], 1)

        @block.scalar
        def _(act):
            A = nc.scalar.activation

            def root_of_norm(n_full, n):
                act.wait_ge(full[6], n_full)
                A(root[:], ps[:, 6, :], ACT.Sqrt, bias=eps[:], scale=1.0 / D_MODEL)
                nc.scalar.drain()
                act.sem_inc(free[6], 1)
                act.sem_inc(root_ready, 1)

            def make_h(L, half, gain):
                sh, sc = (SHIFT_A, SCALE_A) if half == 0 else (SHIFT_F, SCALE_F)
                act.wait_ge(mod_ready, N_MOD * L + sc + 1)
                for k in range(KD):
                    n = 16 * L + 8 * half + k
                    act.wait_ge(xn_ready, n + 1)
                    if n >= 2:
                        act.wait_ge(h_ready, n - 1)
                    for s in range(NSEQ):
                        c = slice(s * SEQ, (s + 1) * SEQ)
                        A(hf[:, k % 2, c], xn[:, k % 2, c], ACT.Identity, bias=mod[:, sh, k, s:s + 1],
                          scale=mod[:, sc, k, s:s + 1])
                    nc.scalar.drain()
                    nc.scalar.copy(h_hi[:, k, :], hf[:, k % 2, :]).then_inc(h_hi_ready, 1)

            def square_x(k, n):
                A(sq_x[:, n % 2, :], x[:, k, :], ACT.Square).then_inc(sq_ready, 1)

            def hi_slot(j, n, landed):
                act.wait_ge(slot_free, n + 1)
                act.wait_ge(raw_landed[j], landed)
                nc.scalar.copy(w_hi[:, j, :], w_raw[:, j, :]).then_inc(hi_done, 1)

            def split_hi(L, s):
                n = L * SLOTS + s
                if n < DEPTH * SLOTS:
                    hi_slot(n % RING, n, 16 * (n // RING + 1))

            def stats(g, s):
                for t in (2 * s, 2 * s + 1):
                    A(junk_o[:], o_sb[:, t, 512 * g:512 * g + 512], ACT.Square, scale=512 ** -0.5,
                      accum_out=st_o[:, 0, 2 * t + g:2 * t + g + 1])
                    nc.scalar.drain()

            act.wait_ge(c_landed, 16)
            A(cact[:], cact[:], ACT.Silu).then_inc(c_ready, 1)
            act.wait_ge(loaded, 16 * N_LOADS)
            act.wait_ge(const_ready, 1)
            for k in range(KD):
                if k >= 2:
                    act.wait_ge(sq_q, k - 1)
                square_x(k, k)
            for b in range(2):
                act.wait_ge(full[b], 1)
                nc.scalar.copy(shift_row[:, b * 512:(b + 1) * 512], ps[0:NSEQ, b, :])
            nc.scalar.drain()
            act.sem_inc(row_ready, 1)
            for b in range(2):
                act.sem_inc(free[b], 1)
            for s in range(3):
                split_hi(0, s)

            for L in range(DEPTH):
                root_of_norm(L * USES[6] + USE["norm1"][1] + 1, 2 * L)
                make_h(L, 0, None)
                split_hi(L, 3)
                for c, (col, width) in enumerate(CHUNKS):
                    for t in range(TT):
                        wait_full(act, L, ("proj", c, t))
                        nc.scalar.copy(proj[:, t, col:col + width], ps[:, t, 0:width]).then_inc(free[t], 1)
                    if c == 1:
                        nc.scalar.drain()
                        for t in range(TT):
                            A(junk[:, 0:Q_LORA], proj[:, t, C_CQ:C_CQ + Q_LORA], ACT.Square, scale=Q_LORA ** -0.5,
                              accum_out=st_lat[:, 0, t:t + 1])
                            nc.scalar.drain()
                            A(junk[:, 0:KV_LORA], proj[:, t, C_CKV:C_CKV + KV_LORA], ACT.Square,
                              scale=KV_LORA ** -0.5, accum_out=st_lat[:, 0, 4 + t:5 + t])
                            nc.scalar.drain()
                        A(st_lat[:, 1, :], st_lat[:, 0, :], ACT.Sqrt, bias=eps[:]).then_inc(lat_sq, 1)
                    if c >= 2:
                        w, h0, nh = QK_BLOCKS[c - 2]
                        n = len(QK_BLOCKS) * L + c - 2
                        nc.scalar.drain()
                        A(sq_qk[:, :, 0:nh * HD], proj[:, :, C_Q + h0 * HD:C_Q + (h0 + nh) * HD],
                          ACT.Square).then_inc(qk_sq, 1)
                        act.wait_ge(qk_ms, n + 1)
                        A(qk_stat(1, h0, nh), qk_stat(0, h0, nh), ACT.Sqrt, bias=eps[:],
                          scale=1.0 / HD).then_inc(qk_root, 1)
                    if c < len(CHUNKS) - 1:
                        for s in range(2):
                            split_hi(L, 2 * c + 4 + s)
                for j in range(3):
                    wait_full(act, L, ("lat", j))
                    A(ct_hi[:, j, :], ps[:, 4 + j, :], ACT.Identity,
                      scale=par[:, L, PC_GCQ + j:PC_GCQ + j + 1]).then_inc(ct_hi_ready, 1)
                for s in range(2):
                    split_hi(L, S_UQ + 2 + s)
                for s in range(4):
                    for t in range(TT):
                        wait_full(act, L, ("uq", s, t))
                        nc.scalar.copy(qb[:, t, 2 * s:2 * s + 2, :],
                                       ps[:, t, 0:2 * QK_B].rearrange("p (h d) -> p h d", h=2)).then_inc(free[t], 1)
                    split_hi(L, S_UQ + 4 + s)
                for s in range(2):
                    for t in range(TT):
                        wait_full(act, L, ("ukv", s, t))
                        if s == 0:
                            nc.scalar.copy(kb[:, t, :, 0:NOPE],
                                           ps[:, t, :].rearrange("p (h d) -> p h d", h=HEADS)).then_inc(free[t], 1)
                        else:
                            nc.scalar.copy(vb[:, t, :], ps[:, t, :]).then_inc(free[t], 1)
                    if s == 0:
                        split_hi(L, S_UKV + 4)
                wait_full(act, L, "kat")
                nc.scalar.copy(ka_t[:], ps[:, 7, :])
                nc.scalar.drain()
                act.sem_inc(free[7], 1)
                act.sem_inc(ka_ready, 1)
                for i in range(-1, NU):
                    if i + 1 < NU and UNITS[i + 1][3]:
                        u = i + 1
                        b, buf = bank(("qt", u)), QT_BUF(u)
                        wait_full(act, L, ("qt", u))
                        last_reader = QT_LAST_READER(u)
                        if last_reader is not None:
                            wait_full(act, L, ("s", last_reader))
                        if UNITS[u][0] == "a":
                            nc.scalar.copy(qk_t[:, buf, 0:SEQ], ps[:, b, 0:SEQ])
                        else:
                            nc.scalar.copy(qk_t[0:QK_B, buf, :], ps[0:QK_B, b, :])
                        nc.scalar.drain()
                        act.sem_inc(free[b], 1)
                        act.sem_inc(qt_ready, 1)
                    if i >= 0:
                        d = HD if UNITS[i][0] == "a" else QK_B
                        act.wait_ge(max_ready, L * NU + i + 1)
                        if i >= 2:
                            wait_full(act, L, ("pt", i - 2))
                        for q in range(2):
                            A(prob[:, i % 2, q, :], ps[:, i % 2, q * SEQ:(q + 1) * SEQ], ACT.Exp,
                              bias=nmx[:, i, q:q + 1], scale=d ** -0.5, accum_out=sme[:, i, q:q + 1])
                        nc.scalar.drain()
                        act.sem_inc(free[i % 2], 1)
                        act.sem_inc(exp_ready, 1)
                        if i in STATS_AT_UNIT:
                            g, s = STATS_AT_UNIT[i]
                            key = ("o", 16 * g + 8 * s + 7)
                            act.wait_ge(free[bank(key)], n_use(L, key) + 1)
                            stats(g, s)
                act.wait_ge(free[bank(("o", NU - 1))], n_use(L, ("o", NU - 1)) + 1)
                stats(1, 1)
                A(st_o[:, 1, :], st_o[:, 0, :], ACT.Sqrt, bias=eps[:]).then_inc(o_root, 1)
                for k in range(KD):
                    wait_full(act, L, ("ot", k))
                    A(h_hi[:, k, :], ps[:, k % 4, :], ACT.Identity,
                      scale=par[:, L, PC_GOUT + k:PC_GOUT + k + 1]).then_inc(ot_hi_ready, 1)
                split_hi(L, S_WO + 3)
                for m in range(KD):
                    n = KD + 2 * KD * L + m
                    act.wait_ge(x_upd, 2 * KD * L + m + 1)
                    act.wait_ge(sq_q, n - 1)
                    square_x(m, n)
                    if m < KD - 1:
                        split_hi(L, S_WO + 4 + m)
                root_of_norm(L * USES[6] + USE["norm2"][1] + 1, 2 * L + 1)
                make_h(L, 1, None)
                split_hi(L, S_WO + 4 + KD - 1)
                for g, n in enumerate(GROUPS):
                    first = sum(GROUPS[:g])
                    with act.Fori(0, n // 2) as it:
                        for e in range(2):
                            tile = L * FT + first + e
                            for half in range(2):
                                ft = 2 * it + (half * FT + first + e)
                                key = ("up", g, e, half)
                                act.wait_ge(full[bank(key)], it + (n_use(L, key) + 1))
                                A(u_sb[:, e, half, :], ps[:, bank(key), :], ACT.Identity,
                                  bias=par[:, L, bass.ds(ft + PC_CB, 1)],
                                  scale=par[:, L, bass.ds(ft + (PC_CW + 2 * FT), 1)]).then_inc(mid_tap, 1)
                            act.wait_ge(taps_done, 2 * it + (tile + 1))
                            A(sil[:, e, :], u_sb[:, e, 1, :], ACT.Silu).then_inc(sil_ready, 1)
                            act.wait_ge(af_ready, 2 * it + (tile + 1))
                            nc.scalar.copy(a_hi[:, bass.ds(2 * it + e, 1), :], af[:, e:e + 1, :]).then_inc(a_hi_ready, 1)
                            for half in range(2):
                                n0 = L * SLOTS + S_UP[g] + 4 + 2 * e + half
                                hi_slot(n0 % RING, RING * it + n0, 16 * it + 16 * (n0 // RING + 1))
                    if g < len(GROUPS) - 1:
                        with act.Fori(0, KD // 4) as it:
                            for e in range(4):
                                n0 = L * SLOTS + S_DOWN[g] + 4 + e
                                hi_slot(n0 % RING, RING * it + n0, 16 * it + 16 * (n0 // RING + 1))
                    else:
                        for m in range(KD):
                            if m < KD - 1:
                                split_hi(L, S_DOWN[g] + 4 + m)
                            n = KD + 2 * KD * L + KD + m
                            act.wait_ge(x_upd, 2 * KD * L + KD + m + 1)
                            act.wait_ge(sq_q, n - 1)
                            square_x(m, n)
            root_of_norm(DEPTH * USES[6] + 1, 2 * DEPTH)

        @block.vector
        def _(dve):
            V = nc.vector

            def ada_start(n_vec):
                if n_vec >= 2:
                    L, v = divmod(n_vec - 1, N_MOD)
                    if n_vec == 2:
                        dve.wait_ge(full[7], 2)
                    else:
                        wait_full(dve, L if v >= 2 else L - 1, ("mod", v))
                V.memset(ada_acc[:], 0.0)
                V.drain()

            def ada_slot(n_vec, kt, plus=None):
                dve.wait_ge(ada_landed[kt % 4], 16 * (2 * (n_vec - 1) + kt // 4 + 1))
                for s in range(NSEQ):
                    V.scalar_tensor_tensor(out=ada_acc[:, s, :], in0=ada_raw[:, kt % 4, :], scalar=cact[:, kt, s:s + 1],
                                           in1=ada_acc[:, s, :], op0=ALU.mult, op1=ALU.add)
                V.drain()
                dve.sem_inc(ada_used, 1)
                if kt == KD - 1:
                    dve.sem_inc(acc_ready, 1)

            def ada_finish(n_vec):
                L, v = divmod(n_vec, N_MOD)
                if n_vec < 2:
                    dve.wait_ge(full[7], n_vec + 1)
                else:
                    wait_full(dve, L if v >= 2 else L - 1, ("mod", v))
                bias = par[:, L, PC_BADA + v * KD:PC_BADA + (v + 1) * KD]
                V.tensor_tensor(mod[:, v, :, :], ps[:, 7, 0:2 * KD].rearrange("p (k s) -> p k s", s=2),
                                bias.rearrange("p (k o) -> p k o", o=1).broadcast_to([P, KD, NSEQ]), ALU.add)
                V.drain()
                if v in (SCALE_A, SCALE_F):
                    g0 = PC_GATTN if v == SCALE_A else PC_GFFN
                    V.tensor_scalar(mod[:, v, :, :], mod[:, v, :, :], 1.0, None, ALU.add)
                    V.drain()
                    V.tensor_tensor(mod[:, v, :, :], mod[:, v, :, :],
                                    par[:, L, g0:g0 + KD].rearrange("p (k o) -> p k o", o=1).broadcast_to([P, KD, NSEQ]),
                                    ALU.mult)
                    V.drain()
                dve.sem_inc(free[7], 1)
                dve.sem_inc(mod_ready, 1)

            def normalise(L, half):
                dve.wait_ge(root_ready, 2 * L + half + 1)
                V.reciprocal(rstd[:], root[:])
                V.drain()

                def lo(k):
                    n = 16 * L + 8 * half + k
                    dve.wait_ge(h_hi_ready, n + 1)
                    V.tensor_tensor(h_lo[:, k, :], hf[:, k % 2, :], h_hi[:, k, :].bitcast(F32),
                                    ALU.subtract).then_inc(h_ready, 1)

                for k in range(KD):
                    V.tensor_tensor(xn[:, k % 2, :], x[:, k, :], rstd[:], ALU.mult).then_inc(xn_ready, 1)
                    if k >= 1:
                        lo(k - 1)
                lo(KD - 1)

            def add_square(n):
                dve.wait_ge(sq_ready, n + 1)
                V.tensor_tensor(ssum[:], ssum[:], sq_x[:, n % 2, :], ALU.add)
                V.drain()
                dve.sem_inc(sq_q, 1)

            def update_x(L, key, k, v, plus=0, done=True):
                wait_full(dve, L, key, plus)
                for s in range(NSEQ):
                    c = slice(s * SEQ, (s + 1) * SEQ)
                    if type(k) is int:
                        xs, gate = x[:, k, c], mod[:, v, k, s:s + 1]
                    else:
                        xs, gate = x[:, bass.ds(k, 1), c], mod[:, v, bass.ds(k, 1), s]
                    V.scalar_tensor_tensor(out=xs, in0=ps[:, bank(key), c], scalar=gate, in1=xs,
                                           op0=ALU.mult, op1=ALU.add)
                V.drain()
                dve.sem_inc(free[bank(key)], 1)
                if done:
                    dve.sem_inc(x_upd, 1)

            dve.sem_inc(ada_used, 4)
            dve.wait_ge(c_ready, 1)
            V.memset(ssum[:], 0.0)
            ada_start(1)
            for kt in range(KD):
                ada_slot(1, kt)
            dve.wait_ge(const_ready, 1)
            for k in range(KD):
                add_square(k)
            dve.sem_inc(ssum_ready, 1)
            ada_finish(0)
            ada_finish(1)

            for L in range(DEPTH):
                n0 = N_MOD * L
                normalise(L, 0)
                for w in range(2):
                    g = gqk[:, L, w:w + 1, :]
                    V.tensor_tensor(cg[:, w], cos_a, g.broadcast_to([P, 2, HD]), ALU.mult)
                    for hf_ in range(2):
                        def quarter(ap, f):
                            return ap.rearrange("p e (s f d) -> p e s f d", s=2, f=2)[:, :, :, f, :]
                        V.tensor_tensor(quarter(sg_t[:, w], hf_), quarter(sin_a, hf_),
                                        quarter(g, 1 - hf_).broadcast_to([P, 2, 2, HD // 4]), ALU.mult)
                ada_start(n0 + GATE_A)
                for kt in range(4):
                    ada_slot(n0 + GATE_A, kt)
                dve.wait_ge(lat_sq, L + 1)
                V.reciprocal(st_lat[:, 0, :], st_lat[:, 1, :])
                V.drain()
                for t in range(TT):
                    V.tensor_scalar(proj[:, t, C_CQ:C_CKV], proj[:, t, C_CQ:C_CKV], st_lat[:, 0, t:t + 1], None, ALU.mult)
                    V.tensor_scalar(proj[:, t, C_CKV:C_KR], proj[:, t, C_CKV:C_KR], st_lat[:, 0, 4 + t:5 + t], None,
                                    ALU.mult)
                V.drain()
                dve.sem_inc(lat_ready, 1)
                kr = proj[:, :, C_KR:C_KR + ROT]
                for e in range(2):
                    for f in range(2):
                        V.tensor_tensor(rot_view(kr_tmp[:, e::2, :], f), rot_view(kr[:, e::2, :], 1 - f),
                                        rot_view(sin_b[:, e:e + 1, :], f).broadcast_to([P, 2, 2, ROT // 4]), ALU.mult)
                for e in range(2):
                    V.tensor_tensor(kr_rot[:, e::2, :], kr[:, e::2, :], cos_b[:, e:e + 1, :].broadcast_to([P, 2, ROT]),
                                    ALU.mult)
                V.drain()
                V.tensor_tensor(kr_rot[:], kr_rot[:], kr_tmp[:], ALU.add).then_inc(kr_ready, 1)
                for kt in range(4, 6):
                    ada_slot(n0 + GATE_A, kt)
                for n, (w, h0, nh) in enumerate(QK_BLOCKS, len(QK_BLOCKS) * L):
                    dve.wait_ge(qk_sq, n + 1)
                    V.tensor_reduce(out=qk_stat(0, h0, nh),
                                    in_=sq_qk[:, :, 0:nh * HD].rearrange("p t (h d) -> p t h d", d=HD),
                                    op=ALU.add, axis=AX_X)
                    V.drain()
                    dve.sem_inc(qk_ms, 1)
                    blk = proj[:, :, C_Q + h0 * HD:C_Q + (h0 + nh) * HD]
                    for t in range(TT):
                        for f in range(2):
                            def view(ap, f):
                                return ap.rearrange("p (h s f d) -> p h s f d", s=2, f=2, d=HD // 4)[:, :, :, f, :]
                            tb = sg_t[:, w, t % 2:t % 2 + 1, :].rearrange("p o (s f d) -> p o s f d", s=2, f=2)[:, :, :, f, :]
                            V.tensor_tensor(view(rope_tmp[:, t, 0:nh * HD], f), view(blk[:, t, :], 1 - f),
                                            tb.broadcast_to([P, nh, 2, HD // 4]), ALU.mult)
                    V.drain()
                    for t in range(TT):
                        xv = blk[:, t, :].rearrange("p (h d) -> p h d", d=HD)
                        V.tensor_tensor(xv, xv, cg[:, w, t % 2:t % 2 + 1, :].broadcast_to([P, nh, HD]), ALU.mult)
                    V.drain()
                    V.tensor_tensor(blk, blk, rope_tmp[:, :, 0:nh * HD], ALU.add)
                    dve.wait_ge(qk_root, n + 1)
                    V.reciprocal(qk_stat(0, h0, nh), qk_stat(1, h0, nh))
                    V.drain()
                    blk4 = blk.rearrange("p t (h d) -> p t h d", d=HD)
                    V.tensor_tensor(blk4, blk4, st_qk[:, 0, :].rearrange("p (t h o) -> p t h o", t=TT, o=1)[
                        :, :, h0:h0 + nh, :].broadcast_to([P, TT, nh, HD]), ALU.mult)
                    V.drain()
                    dve.sem_inc(qk_ready, 1)
                for j in range(3):
                    dve.wait_ge(ct_hi_ready, 3 * L + j + 1)
                    V.scalar_tensor_tensor(out=ct_lo[:, j, :], in0=ps[:, 4 + j, :],
                                           scalar=par[:, L, PC_GCQ + j:PC_GCQ + j + 1],
                                           in1=ct_hi[:, j, :].bitcast(F32), op0=ALU.mult, op1=ALU.subtract)
                    V.drain()
                    dve.sem_inc(free[4 + j], 1)
                    dve.sem_inc(ct_ready, 1)
                for i in range(NU + 2):
                    if i < NU:
                        d = HD if UNITS[i][0] == "a" else QK_B
                        wait_full(dve, L, ("s", i))
                        V.tensor_reduce(out=mx[:, i, :], in_=ps[:, i % 2, :].rearrange("p (q k) -> p q k", q=2),
                                        op=ALU.max, axis=AX_X)
                        V.drain()
                        V.tensor_scalar(nmx[:, i, :], mx[:, i, :], -d ** -0.5, None, ALU.mult).then_inc(max_ready, 1)
                    if 0 <= i - 1 < NU:
                        u = i - 1
                        wait_full(dve, L, ("pt", u))
                        if u >= 2:
                            wait_full(dve, L, ("o", u - 2))
                        V.tensor_copy(prob_t[:, u % 2, :, :], ps[:, 2 + u % 2, :].rearrange("p (a b) -> p a b", a=2))
                        V.reciprocal(rin[:, u, :], sme[:, u, :])
                        V.drain()
                        dve.sem_inc(free[2 + u % 2], 1)
                        dve.sem_inc(pt_ready, 1)
                    if 0 <= i - 2 < NU:
                        u = i - 2
                        group, s, h, _ = UNITS[u]
                        b = bank(("o", u))
                        wait_full(dve, L, ("o", u))
                        col = h * HD + (512 if group == "b" else 0)
                        V.tensor_tensor(o_sb[:, 2 * s:2 * s + 2, col:col + HD],
                                        ps[:, b, 0:2 * HD].rearrange("p (q d) -> p q d", q=2),
                                        rin[:, u, :].rearrange("p (q o) -> p q o", o=1).broadcast_to([P, 2, HD]),
                                        ALU.mult).then_inc(free[b], 1)
                    if i == MOD_AT_UNIT:
                        ada_finish(n0 + GATE_A)
                    if i in ADA_AT_UNIT:
                        v, kt = ADA_AT_UNIT[i]
                        if kt == 0:
                            ada_start(n0 + v)
                        ada_slot(n0 + v, kt)
                dve.wait_ge(o_root, L + 1)
                V.reciprocal(st_o[:, 0, :], st_o[:, 1, :])
                V.drain()
                for g in range(2):
                    for t in range(TT):
                        o = o_sb[:, t, 512 * g:512 * g + 512]
                        V.tensor_scalar(o, o, st_o[:, 0, 2 * t + g:2 * t + g + 1], None, ALU.mult)
                    V.drain()
                    dve.sem_inc(o_ready, 1)
                for k in range(KD):
                    dve.wait_ge(ot_hi_ready, KD * L + k + 1)
                    V.scalar_tensor_tensor(out=h_lo[:, k, :], in0=ps[:, k % 4, :],
                                           scalar=par[:, L, PC_GOUT + k:PC_GOUT + k + 1],
                                           in1=h_hi[:, k, :].bitcast(F32), op0=ALU.mult, op1=ALU.subtract)
                    V.drain()
                    dve.sem_inc(free[k % 4], 1)
                    dve.sem_inc(ot_ready, 1)
                V.memset(ssum[:], 0.0)
                V.drain()
                n_sq = KD + 2 * KD * L
                for m in range(KD):
                    update_x(L, ("wo", m), m, GATE_A)
                    if m >= 1:
                        add_square(n_sq + m - 1)
                    for v, kt in ADA_AT_WO.get(m, []):
                        if kt == 0:
                            ada_finish(n0 + v - 1)
                            ada_start(n0 + v)
                        ada_slot(n0 + v, kt)
                add_square(n_sq + KD - 1)
                dve.sem_inc(ssum_ready, 1)
                ada_finish(n0 + SCALE_F)
                normalise(L, 1)
                for g, n in enumerate(GROUPS):
                    first = sum(GROUPS[:g])
                    n_vec = n0 + GATE_F + g
                    ada = g == 0 or L + 1 < DEPTH
                    if ada:
                        ada_start(n_vec)

                    def tile(i, quad, ada_kt):
                        e = i % 2
                        at = 4 * quad + (first + i)
                        for half in range(2):
                            key = ("up", g, i, half)
                            b = bank(key)
                            dve.wait_ge(mid_tap, 8 * quad + (2 * (L * FT + first + i) + half + 1))
                            for tap, (dst, src) in ((0, (1, 0)), (2, (0, 1))):
                                u3 = u_sb[:, e, half, :].rearrange("p (s t) -> p s t", s=2)
                                p3 = ps[:, b, :].rearrange("p (s t) -> p s t", s=2)
                                V.scalar_tensor_tensor(
                                    out=u3[:, :, dst:dst + SEQ - 1], in0=p3[:, :, src:src + SEQ - 1],
                                    scalar=par[:, L, bass.ds(at + (PC_CW + tap * 2 * FT + half * FT), 1)],
                                    in1=u3[:, :, dst:dst + SEQ - 1], op0=ALU.mult, op1=ALU.add)
                                V.drain()
                            dve.sem_inc(free[b], 1)
                        dve.sem_inc(taps_done, 1)
                        if ada_kt is not None:
                            ada_slot(*ada_kt)
                        dve.wait_ge(sil_ready, 4 * quad + (L * FT + first + i + 1))
                        V.tensor_tensor(af[:, e, :], sil[:, e, :], u_sb[:, e, 0, :], ALU.mult)
                        V.drain()
                        dve.sem_inc(af_ready, 1)
                        dve.wait_ge(a_hi_ready, 4 * quad + (L * FT + first + i + 1))
                        lo_at = bass.ds(4 * quad + i, 1)
                        V.tensor_tensor(a_lo[:, lo_at, :], af[:, e:e + 1, :], a_hi[:, lo_at, :].bitcast(F32),
                                        ALU.subtract).then_inc(a_ready, 1)

                    for quad in range((n + 3) // 4):
                        for i in range(min(4, n - 4 * quad)):
                            tile(i, quad, (n_vec, 4 * quad + i) if ada else None)
                    if ada:
                        for kt in range(n, KD):
                            ada_slot(n_vec, kt)
                        ada_finish(n_vec)
                    if g == len(GROUPS) - 1:
                        V.memset(ssum[:], 0.0)
                        V.drain()
                    n_sq = 2 * KD + 2 * KD * L
                    for m in range(KD):
                        update_x(L, ("down", g, m), m, GATE_F, done=g == len(GROUPS) - 1)
                        if g == len(GROUPS) - 1 and m >= 1:
                            add_square(n_sq + m - 1)
                add_square(n_sq + KD - 1)
                dve.sem_inc(ssum_ready, 1)
            dve.wait_ge(root_ready, 2 * DEPTH + 1)
            V.reciprocal(rstd[:], root[:])
            V.drain()
            for k in range(KD):
                V.scalar_tensor_tensor(out=x[:, k, :], in0=x[:, k, :], scalar=gfin[:, k:k + 1], in1=rstd[:],
                                       op0=ALU.mult, op1=ALU.mult).then_inc(y_done, 1)


SHIFT0 = (DEPTH * N_MOD - 1) * KD

_BLOCKS = [u for u in range(NU) if UNITS[u][3]]


def _block_of(u):
    return max(n for n, first in enumerate(_BLOCKS) if first <= u)


def QT_BUF(u):
    return _block_of(u) % 2


def QT_DONE(L, u):
    return L * len(_BLOCKS) + _block_of(u) + 1


def QT_LAST_READER(u):
    n = _block_of(u)
    return _BLOCKS[n - 1] - 1 if n >= 2 else None


def _tables():
    out = []
    for d in (HD, ROT):
        q = d // 4
        t = np.arange(SEQ)
        pos = np.stack([t // GRID_W, t % GRID_W], -1).astype(np.float32)
        inv = np.float32(THETA) ** (-np.arange(q, dtype=np.float32) / np.float32(q))
        ang = (pos[:, :, None] * inv).astype(np.float32)
        c, s = np.cos(ang), np.sin(ang)
        cos = np.stack([c, c], 2).reshape(2, P, d).transpose(1, 0, 2).reshape(P, 2 * d)
        sin = np.stack([-s, s], 2).reshape(2, P, d).transpose(1, 0, 2).reshape(P, 2 * d)
        out.append(np.stack([cos, sin], 1))
    return np.ascontiguousarray(np.concatenate(out, -1), np.float32)


def _columns(v, n):
    return np.moveaxis(v.reshape(*v.shape[:-1], n, P), -1, 0)


def _pack(inp):
    f = {k: np.asarray(v) for k, v in inp.items()}
    xs = np.concatenate([f["x_prompt"].reshape(SEQ, D_MODEL), f["x_sample"].reshape(SEQ, D_MODEL)], 0)
    x_t = xs.T.reshape(KD, P, T).transpose(1, 0, 2)
    cs = np.concatenate([f["c_prompt"], f["c_sample"]], 0)
    c_t = cs.reshape(NSEQ, KD, P).transpose(2, 1, 0)
    ada = f["w_ada"].reshape(DEPTH, KD, P, N_MOD, SLOT).transpose(0, 3, 1, 2, 4).reshape(DEPTH * N_MOD * KD, P, SLOT)
    ada = np.concatenate([ada[KD:], ada[:KD]], 0)
    slots = np.zeros((DEPTH, SLOTS, P, SLOT), np.float32)
    w_in = f["w_in"]
    wa, kva = HEADS * HD, KV_HEADS * HD
    order = []
    base_cq = wa + 2 * kva
    order += list(range(base_cq, base_cq + Q_LORA + KV_LORA + ROT))
    for p in range(4):
        for g in range(2):
            order += list(range((p + 4 * g) * HD, (p + 4 * g + 1) * HD))
    order += list(range(wa, wa + 2 * kva))
    w_in = w_in[:, :, order]
    for c, (col, width) in enumerate(CHUNKS):
        v = w_in[:, :, col:col + width].reshape(DEPTH, 2, 4, P, width).transpose(0, 1, 3, 2, 4)
        slots[:, S_IN + 2 * c:S_IN + 2 * c + 2, :, 0:4 * width] = v.reshape(DEPTH, 2, P, 4 * width)
    width = 2 * QK_B
    v = f["w_uq"].reshape(DEPTH, 2, P, 4, width).transpose(0, 3, 2, 1, 4)
    slots[:, S_UQ:S_UQ + 4, :, 0:2 * width] = v.reshape(DEPTH, 4, P, 2 * width)
    v = f["w_ukv"].reshape(DEPTH, P, HEADS, 2, HD).transpose(0, 3, 1, 2, 4)
    slots[:, S_UKV:S_UKV + 2, :, 0:HEADS * HD] = v.reshape(DEPTH, 2, P, HEADS * HD)

    def by_column_tile(w, k):
        n = w.shape[2] // P
        return w.reshape(DEPTH, k, P, n, P).transpose(0, 3, 2, 1, 4).reshape(DEPTH, n, P, k * P)

    slots[:, S_WO:S_WO + KD] = by_column_tile(f["w_o"], KD)
    up = by_column_tile(f["w_up"], KD)
    first = 0
    for g, n in enumerate(GROUPS):
        s = S_UP[g]
        slots[:, s:s + 2 * n:2] = up[:, first:first + n]
        slots[:, s + 1:s + 2 * n:2] = up[:, FT + first:FT + first + n]
        s = S_DOWN[g]
        slots[:, s:s + KD, :, 0:n * P] = by_column_tile(f["w_down"][:, first * P:(first + n) * P], n)
        first += n
    par = [_columns(f["g_attn"], KD), _columns(f["g_ffn"], KD),
           _columns(f["g_out_a"], KD // 2), _columns(f["g_out_b"], KD // 2),
           _columns(f["g_cq"], 2), _columns(f["g_ckv"], 1), _columns(f["b_ada"], N_MOD * KD),
           _columns(f["conv_w"], 2 * FT).reshape(P, DEPTH, 6 * FT), _columns(f["conv_b"], 2 * FT)]
    gqk = np.stack([f["g_q_a"], f["g_k_a"]], 1)
    ins = {
        "x_t": x_t, "c_t": c_t, "w_slots": slots.reshape(DEPTH * SLOTS, P, SLOT), "ada_slots": ada,
        "params": np.concatenate(par, -1), "g_qk": np.broadcast_to(gqk, (P, *gqk.shape)),
        "g_fin": _columns(f["g_final"], KD), "tables": _tables(), "ident": np.eye(P, dtype=np.float32),
    }
    return {k: np.ascontiguousarray(v) for k, v in ins.items()}


def kernel(**inputs):
    import concourse.bacc as bacc
    from concourse.bass_utils import run_bass_kernel_spmd

    arrays = _pack(inputs)
    nc = bacc.Bacc("TRN2", target_bir_lowering=False, num_devices=1)
    args = [nc.dram_tensor(k, v.shape, F32, kind="ExternalInput").ap() for k, v in arrays.items()]
    y = nc.dram_tensor("y_t", (P, KD, T), F32, kind="ExternalOutput").ap()
    encoder_kernel(nc, *args, y)
    r = run_bass_kernel_spmd(nc, [arrays], core_ids=[0])
    y = np.asarray(r.results[0]["y_t"]).transpose(2, 1, 0).reshape(NSEQ, SEQ, D_MODEL)
    return y[0:1], y[1:2]
```

```python
from contextlib import ExitStack

import concourse.bass as bass
import numpy as np
from concourse import mybir

F32 = mybir.dt.float32
F32R = mybir.dt.float32r
ALU = mybir.AluOpType
ACT = mybir.ActivationFunctionType
AX_X = mybir.AxisListType.X

P = 128
D_MODEL = 1024
DEPTH = 2
SEQ = 256
NSEQ = 2
T = NSEQ * SEQ
TT = T // P
KD = D_MODEL // P
GRID_W = 64
THETA = 10000.0
EPS = 1e-6
HEADS = 8
HD = 64
KV_HEADS = 2
NOPE = 64
ROT = 32
QK_B = NOPE + ROT
Q_LORA = 256
KV_LORA = 128
D_FF = 2816
FT = D_FF // P
N_MOD = 6

C_CQ = 0
C_CKV = C_CQ + Q_LORA
C_KR = C_CKV + KV_LORA
C_Q = C_KR + ROT
C_K = C_Q + HEADS * HD
C_V = C_K + KV_HEADS * HD
D_IN = C_V + KV_HEADS * HD
CHUNKS = [(C_CQ, 256), (C_CKV, 160), (C_Q, 256), (C_Q + 256, 256), (C_K, 256)]

SLOT = 1024
RING = 4
GROUPS = [8, 8, 6]
S_IN = 0
S_UQ = S_IN + 2 * len(CHUNKS)
S_UKV = S_UQ + 4
S_WO = S_UKV + 2
S_FFN = S_WO + KD
S_UP, S_DOWN = [], []
_at = S_FFN
for _n in GROUPS:
    S_UP.append(_at)
    S_DOWN.append(_at + 2 * _n)
    _at += 2 * _n + KD
SLOTS = _at
ROUNDS = SLOTS // RING
assert SLOTS % RING == 0 and sum(GROUPS) == FT

PC_GATTN = 0
PC_GFFN = PC_GATTN + KD
PC_GOUT = PC_GFFN + KD
PC_GCQ = PC_GOUT + KD
PC_GCKV = PC_GCQ + 2
PC_BADA = PC_GCKV + 1
PC_CW = PC_BADA + N_MOD * KD
PC_CB = PC_CW + 3 * 2 * FT
NPC = PC_CB + 2 * FT
SHIFT_A, SCALE_A, GATE_A, SHIFT_F, SCALE_F, GATE_F = range(N_MOD)

UNITS = [("a", s, p + 4 * g, g == 0) for s in range(NSEQ) for p in range(4) for g in range(2)]
UNITS += [("b", s, h, True) for s in range(NSEQ) for h in range(HEADS)]
NU = len(UNITS)
QK_BLOCKS = [(0, 0, 4), (0, 4, 4), (1, 8, 2)]


STAGES = ["in", "attn", "wo", "up0", "down0", "up1", "down1", "up2"]


def stage_vectors(L):
    out = {"attn": (L, SCALE_F), "up0": (L, GATE_F)}
    if L == 0:
        out.update({"in": (L, GATE_A), "attn": (L, SHIFT_F), "wo": (L, SCALE_F)})
    if L + 1 < DEPTH:
        out.update({"down0": (L + 1, SHIFT_A), "up1": (L + 1, SCALE_A), "down1": (L + 1, GATE_A), "up2": (L + 1, SHIFT_F)})
    return out


ORDER = [(0, SCALE_A)] + [stage_vectors(L)[st] for L in range(DEPTH) for st in STAGES if st in stage_vectors(L)]
ADA_NUMBER = {v: n for n, v in enumerate(ORDER)}
ADA_AT_UP = [{0: (0, 1), 1: (2, 3), 2: (4,), 3: (5,), 4: (6,), 5: (7,)}] * 2 + [{0: (0, 1), 1: (2, 3), 2: (4, 5), 3: (6, 7)}]
ADA_AT_DOWN = [(), (0, 1), (2, 3), (4,), (5, 6), (7,), (), ()]
LAG_P, LAG_O = 2, 3
ADA_VECTOR_E = 3
NORM_WARM = (8, 14)
WARM_UP = {-1: 14, 0: 12, 1: 8, 2: 6}
STATS_AT_UNIT = {12: (0, 0), 20: (0, 1), 28: (1, 0)}
NORM_A_AT = 24


def plan_banks(L, count):
    use = {}

    def take(key, bank):
        if key[0] == "mod" and key[1] not in stage_vectors(L):
            return
        use[key] = (bank, count[bank])
        count[bank] += 1

    take("norm1", 6)
    take("rstd1", 6)
    for c in range(len(CHUNKS)):
        for t in range(TT):
            take(("proj", c, t), t)
    for j in range(3):
        take(("lat", j), 4 + j)
    for s in range(4):
        for t in range(TT):
            take(("uq", s, t), t)
    for s in range(2):
        for t in range(TT):
            take(("ukv", s, t), t)
    take(("mod", "in"), 7)
    take("kat", 7)
    pairs = 0
    for i in range(-1, NU + LAG_O):
        if i + 1 < NU and UNITS[i + 1][3]:
            take(("qt", i + 1), 4 + pairs % 2)
            pairs += 1
        if 0 <= i < NU:
            take(("s", i), i % 3)
        if 0 <= i - LAG_P < NU:
            take(("pt", i - LAG_P), 3)
        if 0 <= i - LAG_O < NU:
            take(("o", i - LAG_O), 6 + (i - LAG_O) % 2)
    for k in range(KD):
        take(("ot", k), k % 4)
    take(("mod", "attn"), 7)
    for m in range(KD):
        take(("wo", m), 4 + m % 2)
    take(("mod", "wo"), 7)
    take("norm2", 6)
    take("rstd2", 6)
    for g, n in enumerate(GROUPS):
        for i in range(n):
            take(("up", g, i, 0), 2 * (i % 2))
            take(("up", g, i, 1), 2 * (i % 2) + 1)
        take(("mod", f"up{g}"), 7)
        for m in range(KD):
            take(("down", g, m), 4 + m % 2)
        take(("mod", f"down{g}"), 7)
    return use


USES = [1, 1, 0, 0, 0, 0, 0, 2]
USE = [plan_banks(L, USES) for L in range(DEPTH)]


def ada_rounds(L):
    out = {3: 4, 4: 4, 7: 4, 8: 4}
    if L == 0:
        out.update({1: 4, 2: 4, 5: 4, 6: 4})
    if L + 1 < DEPTH:
        out.update({10: 4, 11: 4, 13: 4, 14: 2, 15: 2, 16: 4, 17: 4, 19: 4, 20: 4})
    return out


def encoder_kernel(nc, x_t, c_t, w_slots, ada_slots, params, g_qk, g_fin, tables, ident_d, y_t):
    ctx = ExitStack()
    with ctx:
        base = [16512]

        def sem(name):
            return ctx.enter_context(nc.semaphore(name))

        def put(name, shape, dt=F32, at=None):
            size = 4 * int(np.prod(shape[1:]))
            if at is None:
                at = base[0]
                base[0] += (size + 31) // 32 * 32
            return nc.alloc_sbuf_tensor_at(name, shape, dt, offset=at)

        x = put("x", [P, KD, T])
        at_h = base[0]
        h_hi = put("h_hi", [P, KD, T], F32R)
        h_lo = put("h_lo", [P, KD, T], F32R)
        at_act = base[0]
        a_hi = put("a_hi", [P, 8, T], F32R)
        a_lo = put("a_lo", [P, 8, T], F32R)
        w_raw = put("w_raw", [P, RING, SLOT])
        w_hi = put("w_hi", [P, RING, SLOT], F32R)
        w_lo = put("w_lo", [P, RING, SLOT], F32R)
        ada_raw = put("ada_raw", [P, 4, SLOT])
        ada_acc = put("ada_acc", [P, NSEQ, SLOT])
        at_proj = base[0]
        proj = put("proj", [P, TT, D_IN])
        at_o = base[0]
        o_sb = put("o_sb", [P, TT, D_MODEL])
        rstd_diag = put("rstd_diag", [P, TT, P])
        rstd = put("rstd", [P, TT])
        root = put("root", [P, TT])
        ssum = put("ssum", [P, T])
        mod = put("mod", [P, N_MOD, KD, NSEQ])
        cact = put("cact", [P, KD, NSEQ])
        par = put("par", [P, DEPTH, NPC])
        gqk = put("gqk", [P, DEPTH, 2, HD])
        gfin = put("gfin", [P, KD])
        tab = put("tab", [P, 2, 2 * (HD + ROT)])
        ident = put("ident", [P, P])
        ones = put("ones", [P, P])
        eps = put("eps", [P, 1])
        kr_tmp = put("kr_tmp", [P, TT, ROT])
        kr_rot = put("kr_rot", [P, TT, ROT])
        shift_row = put("shift_row", [NSEQ, SLOT])
        cg = put("cg", [P, 2, 2, HD])
        sg_t = put("sg_t", [P, 2, 2, HD])
        st_lat = put("st_lat", [P, 2, 8])
        st_qk = put("st_qk", [P, 2, 40])
        st_o = put("st_o", [P, 2, 8])
        mx = put("mx", [P, NU, 2])
        nmx = put("nmx", [P, NU, 2])
        sme = put("sme", [P, NU, 2])
        rin = put("rin", [P, NU, 2])
        unread = put("unread", [P, 6 * DEPTH])
        assert base[0] <= nc.sbuf_usable_end, base[0]
        qb = put("qb", [P, TT, HEADS, QK_B], at=at_h)
        shift0 = put("shift0", [P, KD, SLOT], at=at_h)
        kb = put("kb", [P, TT, HEADS, QK_B], at=at_h + 12288)
        vb = put("vb", [P, TT, HEADS * HD], at=at_h + 24576)
        ct_hi = put("ct_hi", [P, 3, T], F32R, at=at_act)
        ct_lo = put("ct_lo", [P, 3, T], F32R, at=at_act + 6144)
        prob = put("prob", [P, 3, 2, SEQ], at=at_act + 2048)
        prob_t = put("prob_t", [P, 2, 2, SEQ], at=at_act + 16384)
        qk_t = put("qk_t", [P, 2, T], at=at_act + 20480)
        ka_t = put("ka_t", [P, T], at=at_act + 24576)
        qb_tmp = put("qb_tmp", [P, TT, HEADS, ROT], at=at_act + 26624)
        ada_part = put("ada_part", [P, SLOT], at=at_act + 26624)
        junk_o = put("junk_o", [P, 512], at=at_act)
        xn = put("xn", [P, 2, T], at=at_o)
        hf = put("hf", [P, 2, T], at=at_o + 4096)
        sq_x = put("sq_x", [P, 2, T], at=at_o + 10240)
        sq_qk = put("sq_qk", [P, TT, 4 * HD], at=at_o)
        rope_tmp = put("rope_tmp", [P, TT, 4 * HD], at=at_o + 4096)
        junk = put("junk", [P, 512], at=at_o + 14336)
        u_sb = put("u_sb", [P, 2, 2, T], at=at_proj)
        sil = put("sil", [P, 2, T], at=at_proj + 8192)
        af = put("af", [P, 2, T], at=at_proj + 12288)
        ps = ctx.enter_context(nc.psum_tensor("ps", [P, 8, 512], F32))

        def qk_stat(r, h0, nh):
            return st_qk[:, r, :].rearrange("p (t h) -> p t h", t=TT)[:, :, h0:h0 + nh]

        cos_a = tab[:, 0, 0:2 * HD].rearrange("p (e d) -> p e d", e=2)
        sin_a = tab[:, 1, 0:2 * HD].rearrange("p (e d) -> p e d", e=2)
        cos_b = tab[:, 0, 2 * HD:].rearrange("p (e d) -> p e d", e=2)
        sin_b = tab[:, 1, 2 * HD:].rearrange("p (e d) -> p e d", e=2)

        c_landed = sem("c_landed")
        shift0_landed = [sem(f"shift0_landed{k}") for k in range(2)]
        row_ready = sem("row_ready")
        loaded = sem("loaded")
        raw_landed = [sem(f"raw_landed{j}") for j in range(RING)]
        raw_free = sem("raw_free")
        hi_done = sem("hi_done")
        split_done = sem("split_done")
        slot_free = sem("slot_free")
        ada_landed = [sem(f"ada_landed{j}") for j in range(4)]
        ada_used = sem("ada_used")
        acc_ready = sem("acc_ready")
        mod_ready = sem("mod_ready")
        c_ready = sem("c_ready")
        full = [sem(f"bank_full{b}") for b in range(8)]
        free = [sem(f"bank_free{b}") for b in range(8)]
        const_ready = sem("const_ready")
        ssum_ready = sem("ssum_ready")
        diag_ready = sem("diag_ready")
        root_ready = sem("root_ready")
        xn_ready = sem("xn_ready")
        h_hi_ready = sem("h_hi_ready")
        h_ready = sem("h_ready")
        sq_q = sem("sq_q")
        lat_sq = sem("lat_sq")
        lat_ready = sem("lat_ready")
        ct_hi_ready = sem("ct_hi_ready")
        ct_ready = sem("ct_ready")
        qk_sq = sem("qk_sq")
        qk_ms = sem("qk_ms")
        qk_root = sem("qk_root")
        qk_ready = sem("qk_ready")
        kr_ready = sem("kr_ready")
        ka_ready = sem("ka_ready")
        b_ready = sem("b_ready")
        qt_ready = sem("qt_ready")
        max_ready = sem("max_ready")
        exp_ready = sem("exp_ready")
        pt_ready = sem("pt_ready")
        o_root = sem("o_root")
        o_ready = sem("o_ready")
        ot_hi_ready = sem("ot_hi_ready")
        ot_ready = sem("ot_ready")
        x_upd = sem("x_upd")
        sq_ready = sem("sq_ready")
        mid_tap = sem("mid_tap")
        taps_done = sem("taps_done")
        sil_ready = sem("sil_ready")
        af_ready = sem("af_ready")
        a_hi_ready = sem("a_hi_ready")
        a_ready = sem("a_ready")
        y_done = sem("y_done")
        stored = sem("stored")

        def bank(key):
            return USE[0][key][0]

        def n_use(L, key):
            return USE[L][key][1]

        def wait_full(eng, L, key, plus=0):
            eng.wait_ge(full[bank(key)], n_use(L, key) + 1 + plus)

        def wait_free(eng, L, key, plus=0):
            n = n_use(L, key) + plus
            if type(n) is not int or n > 0:
                eng.wait_ge(free[bank(key)], n)

        def rot_view(ap, f):
            return ap.rearrange("p t (s f d) -> p t s f d", s=2, f=2)[:, :, :, f, :]

        block = ctx.enter_context(nc.Block())

        N_LOADS = 7

        @block.sync
        def _(sp):
            def load_ada(n_vec, kt):
                sp.wait_ge(ada_used, 8 * n_vec + kt + 1)
                sp.dma_start(ada_raw[:, kt % 4, :], ada_slots[8 * n_vec + kt]).then_inc(ada_landed[kt % 4], 16)

            def load_round(L, r):
                for j in range(RING):
                    sp.wait_ge(raw_free, L * SLOTS + RING * r + j + 1)
                    sp.dma_start(w_raw[:, j, :], w_slots[L * SLOTS + RING * r + j]).then_inc(raw_landed[j], 16)

            sp.dma_start(cact[:], c_t).then_inc(c_landed, 16)
            for half in range(2):
                for kt in range(2):
                    load_ada(0, 4 * half + kt)
                sp.dma_start(shift0[:, 4 * half:4 * half + 4, :],
                             ada_slots[SHIFT0 + 4 * half:SHIFT0 + 4 * half + 4].rearrange("k p n -> p k n")
                             ).then_inc(shift0_landed[half], 16)
                for kt in range(2, 4):
                    load_ada(0, 4 * half + kt)
                sp.dma_start(x[:, 4 * half:4 * half + 4, :], x_t[:, 4 * half:4 * half + 4, :]).then_inc(loaded, 16)
            sp.dma_start(par[:], params).then_inc(loaded, 16)
            sp.dma_start(gqk[:], g_qk).then_inc(loaded, 16)
            sp.dma_start(gfin[:], g_fin).then_inc(loaded, 16)
            sp.dma_start(tab[:], tables).then_inc(loaded, 16)
            sp.dma_start(ident[:], ident_d).then_inc(loaded, 16)
            loaded_ada = [KD]
            for L in range(DEPTH):
                for r in range(ROUNDS):
                    load_round(L, r)
                    for _ in range(ada_rounds(L).get(r, 0)):
                        load_ada(loaded_ada[0] // KD, loaded_ada[0] % KD)
                        loaded_ada[0] += 1
            for k in range(KD):
                sp.wait_ge(y_done, k + 1)
                sp.dma_start(y_t[:, k, :], x[:, k, :]).then_inc(stored, 16)
            sp.wait_ge(stored, 16 * KD)

        @block.gpsimd
        def _(pool):
            nc.gpsimd.memset(ones[:], 1.0)
            nc.gpsimd.memset(eps[:], EPS)
            nc.gpsimd.drain()
            pool.sem_inc(const_ready, 1)
            pool.sem_inc(raw_free, RING)
            pool.wait_ge(c_ready, 1)

            def lo_slot(j, n):
                pool.wait_ge(hi_done, n + 1)
                nc.gpsimd.tensor_tensor(w_lo[:, j, :], w_raw[:, j, :], w_hi[:, j, :].bitcast(F32), ALU.subtract)
                nc.gpsimd.drain()
                pool.sem_inc(raw_free, 1)
                pool.sem_inc(split_done, 1)

            def lo_rounds(L, r0, r1):
                with pool.Fori(0, r1 - r0) as r:
                    for j in range(RING):
                        lo_slot(j, RING * r + (L * SLOTS + RING * r0 + j))

            for L in range(DEPTH):
                lo_rounds(L, 0, S_WO // RING)
                for s in range(S_WO, S_WO + 3):
                    lo_slot(s % RING, L * SLOTS + s)
                pool.wait_ge(kr_ready, L + 1)
                wait_b = ("uq", 3, TT - 1)
                pool.wait_ge(free[bank(wait_b)], n_use(L, wait_b) + 1)
                for t in range(TT):
                    for f in range(2):
                        nc.gpsimd.tensor_tensor(rot_view(qb_tmp[:, t], f), rot_view(qb[:, t, :, NOPE:], 1 - f),
                                                rot_view(sin_b[:, t % 2:t % 2 + 1, :], f).broadcast_to(
                                                    [P, HEADS, 2, ROT // 4]), ALU.mult)
                nc.gpsimd.drain()
                for t in range(TT):
                    nc.gpsimd.tensor_tensor(qb[:, t, :, NOPE:], qb[:, t, :, NOPE:],
                                            cos_b[:, t % 2:t % 2 + 1, :].broadcast_to([P, HEADS, ROT]), ALU.mult)
                    nc.gpsimd.tensor_copy(kb[:, t, :, NOPE:], kr_rot[:, t:t + 1, :].broadcast_to([P, HEADS, ROT]))
                nc.gpsimd.drain()
                nc.gpsimd.tensor_tensor(qb[:, :, :, NOPE:], qb[:, :, :, NOPE:], qb_tmp[:], ALU.add)
                nc.gpsimd.drain()
                pool.sem_inc(b_ready, 1)
                n = ADA_NUMBER[stage_vectors(L)["attn"]]
                pool.wait_ge(ada_used, 4 + KD * n + ADA_VECTOR_E)
                for kt in range(ADA_VECTOR_E, KD):
                    pool.wait_ge(ada_landed[kt % 4], 16 * (2 * n + kt // 4 + 1))
                    for s in range(NSEQ):
                        nc.gpsimd.tensor_scalar(ada_part[:], ada_raw[:, kt % 4, :], cact[:, kt, s:s + 1], None, ALU.mult)
                        nc.gpsimd.drain()
                        nc.gpsimd.tensor_tensor(ada_acc[:, s, :], ada_acc[:, s, :], ada_part[:], ALU.add)
                        nc.gpsimd.drain()
                    pool.sem_inc(ada_used, 1)
                pool.sem_inc(acc_ready, 1)
                lo_slot((S_WO + 3) % RING, L * SLOTS + S_WO + 3)
                lo_rounds(L, S_WO // RING + 1, ROUNDS)

        @block.tensor
        def _(pe):
            mm = nc.tensor.matmul
            pe.sem_inc(slot_free, RING - 1)

            def slot(L, s):
                pe.wait_ge(split_done, L * SLOTS + s + 1)
                return s % RING

            def product(out, stat, mov, first, last, release=0):
                hh = mm(out, stat[0], mov[0], start=first, stop=False)
                hl = mm(out, stat[0], mov[1], start=False, stop=False)
                if release >= 1:
                    hh.then_inc(slot_free, 1)
                if release >= 2:
                    hl.then_inc(slot_free, 1)
                return mm(out, stat[1], mov[0], start=False, stop=last)

            def sum_mod(L, stage):
                if L is not None and stage not in stage_vectors(L):
                    return
                if L is None:
                    pe.wait_ge(acc_ready, 1)
                    pe.wait_ge(free[7], 1)
                else:
                    pe.wait_ge(acc_ready, ADA_NUMBER[stage_vectors(L)[stage]] + 1)
                    wait_free(pe, L, ("mod", stage))
                for j in range(KD):
                    for s in range(NSEQ):
                        last = mm(ps[:, 7, 2 * j + s:2 * j + s + 1], ada_acc[:, s, P * j:P * j + P], ones[:, 0:1],
                                  start=True, stop=True)
                last.then_inc(full[7], 1)

            def keep_warm(b, count):
                for _ in range(count):
                    mm(ps[:, b, 0:P], ones[:], ones[:], start=True, stop=True)

            def norm_sums(L, half):
                n = 2 * L + half
                last_norm = L == DEPTH
                next_key = None if last_norm else [("proj", 0, 0), ("up", 0, 0, 0)][half]
                used = USES[6] if last_norm else n_use(L, f"norm{half + 1}")
                pe.wait_ge(ssum_ready, n + 1)
                if used > 0:
                    pe.wait_ge(free[6], used)
                for t in range(TT):
                    last = mm(ps[:, 6, t:t + 1], ssum[:, t * P:t * P + P], ones[:, 0:1], start=True, stop=True)
                last.then_inc(full[6], 1)
                if next_key:
                    wait_free(pe, L, next_key)
                    keep_warm(bank(next_key), NORM_WARM[0])
                pe.wait_ge(free[6], used + 1)
                pe.wait_ge(diag_ready, n + 1)
                for t in range(TT):
                    last = mm(ps[:, 6, t * P:t * P + P], ones[:], rstd_diag[:, t, :], start=True, stop=True)
                last.then_inc(full[6], 1)
                if next_key:
                    keep_warm(bank(next_key), NORM_WARM[1])

            def output_transposes(L, k):
                pe.wait_ge(o_ready, 2 * L + k // 4 + 1)
                wait_free(pe, L, ("ot", k))
                for t in range(TT):
                    last = nc.tensor.transpose(ps[:, k % 4, t * P:t * P + P], o_sb[:, t, k * P:k * P + P], ident[:])
                last.then_inc(full[k % 4], 1)

            def out_tile(L, m, ks, release):
                j = slot(L, S_WO + m)
                if 0 in ks:
                    wait_free(pe, L, ("wo", m))
                for k in ks:
                    pe.wait_ge(ot_ready, KD * L + k + 1)
                    last = product(ps[:, 4 + m % 2, :], [r[:, j, k * P:k * P + P] for r in (w_hi, w_lo)],
                                   [r[:, k, :] for r in (h_hi, h_lo)], k == 0, k == KD - 1, release * int(k == ks[0]))
                if KD - 1 in ks:
                    last.then_inc(full[4 + m % 2], 1)

            def down_tile(L, g, m, ks, release):
                key = ("down", g, m)
                n = GROUPS[g]
                j = slot(L, S_DOWN[g] + m)
                if 0 in ks:
                    wait_free(pe, L, key)
                for k in ks:
                    if m == 0:
                        pe.wait_ge(a_ready, L * FT + sum(GROUPS[:g]) + k + 1)
                    last = product(ps[:, bank(key), :], [r[:, j, k * P:k * P + P] for r in (w_hi, w_lo)],
                                   [r[:, k, :] for r in (a_hi, a_lo)], k == 0, k == n - 1, release * int(k == ks[0]))
                if n - 1 in ks:
                    last.then_inc(full[bank(key)], 1)

            pe.wait_ge(const_ready, 1)
            pe.wait_ge(c_ready, 1)
            for k in range(KD):
                if k % 4 == 0:
                    pe.wait_ge(shift0_landed[k // 4], 16)
                for b in range(2):
                    last = mm(ps[0:NSEQ, b, :], cact[:, k, :], shift0[:, k, b * 512:(b + 1) * 512], start=(k == 0),
                              stop=(k == KD - 1))
                    if k == KD - 1:
                        last.then_inc(full[b], 1)
            pe.wait_ge(loaded, 16 * N_LOADS)
            pe.wait_ge(row_ready, 1)
            for j in range(KD):
                last = nc.tensor.transpose(ps[:, 7, 2 * j:2 * j + 2], shift_row[:, j * P:(j + 1) * P],
                                           ident[0:NSEQ, 0:NSEQ])
            last.then_inc(full[7], 1)
            sum_mod(None, None)

            for L in range(DEPTH):
                norm_sums(L, 0)
                for c, (col, width) in enumerate(CHUNKS):
                    if c == len(CHUNKS) - 1:
                        pe.wait_ge(lat_ready, L + 1)
                        for j in range(3):
                            wait_free(pe, L, ("lat", j))
                            for t in range(TT):
                                last = nc.tensor.transpose(ps[:, 4 + j, t * P:t * P + P], proj[:, t, j * P:j * P + P], ident[:])
                            last.then_inc(full[4 + j], 1)
                    halves = [0, 0]

                    def part(k, t, first, last, release=0):
                        j = halves[k // 4]
                        w = [r[:, j, (k % 4) * width:(k % 4 + 1) * width] for r in (w_hi, w_lo)]
                        st = [r[:, k, t * P:t * P + P] for r in (h_hi, h_lo)]
                        return product(ps[:, t, 0:width], st, w, first, last, release)

                    if c == 0:
                        for k in range(KD):
                            if k % 4 == 0:
                                halves[k // 4] = slot(L, S_IN + k // 4)
                            pe.wait_ge(h_ready, 16 * L + k + 1)
                            for t in range(TT):
                                if k == 0:
                                    wait_free(pe, L, ("proj", c, t))
                                last = part(k, t, k == 0, k == KD - 1, int(k == 0 and t == 0))
                                if k == KD - 1:
                                    last.then_inc(full[t], 1)
                    else:
                        for t in range(TT):
                            wait_free(pe, L, ("proj", c, t))
                            for k in range(KD):
                                if t == 0 and k % 4 == 0:
                                    halves[k // 4] = slot(L, S_IN + 2 * c + k // 4)
                                last = part(k, t, k == 0, k == KD - 1, 2 * int(k == 0 and t == 0))
                            last.then_inc(full[t], 1)
                width = 2 * QK_B
                for s in range(4):
                    j = slot(L, S_UQ + s)
                    if s == 0:
                        pe.wait_ge(ct_ready, 3 * L + 2)
                    for t in range(TT):
                        wait_free(pe, L, ("uq", s, t))
                        for k in range(2):
                            last = product(ps[:, t, 0:width], [r[:, k, t * P:t * P + P] for r in (ct_hi, ct_lo)],
                                           [r[:, j, k * width:(k + 1) * width] for r in (w_hi, w_lo)], k == 0, k == 1,
                                           (1 + int(s == 0)) * int(k == 0 and t == 0))
                        last.then_inc(full[t], 1)
                pe.wait_ge(ct_ready, 3 * L + 3)
                for s in range(2):
                    j = slot(L, S_UKV + s)
                    for t in range(TT):
                        wait_free(pe, L, ("ukv", s, t))
                        product(ps[:, t, :], [r[:, 2, t * P:t * P + P] for r in (ct_hi, ct_lo)],
                                [r[:, j, 0:512] for r in (w_hi, w_lo)], True, True, int(t == 0)).then_inc(full[t], 1)
                sum_mod(L, "in")
                wait_free(pe, L, "kat")
                pe.wait_ge(qk_ready, len(QK_BLOCKS) * (L + 1))
                for t in range(TT):
                    last = nc.tensor.transpose(ps[:, 7, t * P:t * P + P], proj[:, t, C_K:C_K + P], ident[:])
                last.then_inc(full[7], 1)
                for i in range(-1, NU + LAG_O):
                    if i + 1 < NU and UNITS[i + 1][3]:
                        group, s, h, _ = UNITS[i + 1]
                        b = bank(("qt", i + 1))
                        wait_free(pe, L, ("qt", i + 1))
                        if group == "b" and UNITS[i][0] == "a":
                            pe.wait_ge(b_ready, L + 1)
                        for q in range(2):
                            if group == "a":
                                last = nc.tensor.transpose(ps[:, b, q * P:q * P + P],
                                                           proj[:, 2 * s + q, C_Q + h * P:C_Q + h * P + P], ident[:])
                            else:
                                nc.tensor.transpose(ps[0:QK_B, b, q * P:q * P + P], qb[:, 2 * s + q, h, :], ident[:])
                                last = nc.tensor.transpose(ps[0:QK_B, b, SEQ + q * P:SEQ + q * P + P],
                                                           kb[:, 2 * s + q, h, :], ident[:])
                        last.then_inc(full[b], 1)
                    if i == -1:
                        wait_free(pe, L, ("o", 0))
                    keep_warm(bank(("o", 0)), WARM_UP.get(i, 0))
                    if 0 <= i < NU:
                        group, s, h, _ = UNITS[i]
                        wait_free(pe, L, ("s", i))
                        pe.wait_ge(qt_ready, QT_DONE(L, i))
                        if i == 0:
                            pe.wait_ge(ka_ready, L + 1)
                        buf = QT_BUF(i)
                        for q in range(2):
                            if group == "a":
                                o = 64 * (h // 4)
                                st, mv = qk_t[o:o + 64, buf, q * P:q * P + P], ka_t[o:o + 64, s * SEQ:(s + 1) * SEQ]
                            else:
                                st, mv = qk_t[0:QK_B, buf, q * P:q * P + P], qk_t[0:QK_B, buf, SEQ:2 * SEQ]
                            last = mm(ps[:, i % 3, q * SEQ:(q + 1) * SEQ], st, mv, start=True, stop=True)
                        last.then_inc(full[i % 3], 1)
                    if 0 <= i - LAG_P < NU:
                        u = i - LAG_P
                        wait_free(pe, L, ("pt", u))
                        pe.wait_ge(exp_ready, L * NU + u + 1)
                        for q in range(2):
                            for k in range(2):
                                last = nc.tensor.transpose(
                                    ps[:, 3, k * SEQ + q * P:k * SEQ + q * P + P],
                                    prob[:, u % 3, q, k * P:k * P + P], ident[:])
                        last.then_inc(full[3], 1)
                    if 0 <= i - LAG_O < NU:
                        u = i - LAG_O
                        group, s, h, _ = UNITS[u]
                        b = bank(("o", u))
                        wait_free(pe, L, ("o", u))
                        pe.wait_ge(pt_ready, L * NU + u + 1)
                        for q in range(2):
                            for k in range(2):
                                if group == "a":
                                    v = proj[:, 2 * s + k, C_V + HD * (h // 4):C_V + HD * (h // 4) + HD]
                                else:
                                    v = vb[:, 2 * s + k, h * HD:(h + 1) * HD]
                                last = mm(ps[:, b, q * HD:(q + 1) * HD], prob_t[:, u % 2, k, q * P:q * P + P], v,
                                          start=(k == 0), stop=(k == 1))
                        last.then_inc(full[b], 1)
                    if i >= NU:
                        output_transposes(L, i - NU)
                for k in range(LAG_O, KD // 2):
                    output_transposes(L, k)
                for m in range(2):
                    out_tile(L, m, range(KD // 2), int(m == 0))
                for k in range(KD // 2, KD):
                    output_transposes(L, k)
                sum_mod(L, "attn")
                for m in range(2):
                    out_tile(L, m, range(KD // 2, KD), int(m == 1))
                for m in range(2, KD):
                    out_tile(L, m, range(KD), 1)
                sum_mod(L, "wo")
                norm_sums(L, 1)
                for g, n in enumerate(GROUPS):
                    peeled = 0
                    if g == 0:
                        peeled = 1
                        for k in range(KD):
                            pe.wait_ge(h_ready, 16 * L + 8 + k + 1)
                            for j in range(2):
                                key = ("up", 0, 0, j)
                                if k == 0:
                                    slot(L, S_UP[0] + j)
                                    wait_free(pe, L, key)
                                last = product(ps[:, bank(key), :], [r[:, j, k * P:k * P + P] for r in (w_hi, w_lo)],
                                               [r[:, k, :] for r in (h_hi, h_lo)], k == 0, k == KD - 1,
                                               int((k == 0 and j == 0) or (k == KD - 1 and j > 0)))
                                if k == KD - 1:
                                    last.then_inc(full[bank(key)], 1)
                        for j in range(2, RING):
                            key = ("up", 0, 1, j - 2)
                            slot(L, S_UP[0] + j)
                            wait_free(pe, L, key)
                            for k in range(KD):
                                last = product(ps[:, bank(key), :], [r[:, j, k * P:k * P + P] for r in (w_hi, w_lo)],
                                               [r[:, k, :] for r in (h_hi, h_lo)], k == 0, k == KD - 1, int(k == 0))
                            last.then_inc(full[bank(key)], 1)
                    with pe.Fori(peeled, n // 2) as it:
                        for e in range(2):
                            for half in range(2):
                                key = ("up", g, e, half)
                                pe.wait_ge(split_done, 4 * it + (L * SLOTS + S_UP[g] + 2 * e + half + 1))
                                wait_free(pe, L, key, it)
                                j = (S_UP[g] + 2 * e + half) % RING
                                for k in range(KD):
                                    last = product(ps[:, bank(key), :],
                                                   [r[:, j, k * P:k * P + P] for r in (w_hi, w_lo)],
                                                   [r[:, k, :] for r in (h_hi, h_lo)], k == 0, k == KD - 1, int(k == 0))
                                last.then_inc(full[bank(key)], 1)
                    sum_mod(L, f"up{g}")
                    for m in range(2):
                        down_tile(L, g, m, range(n - 1), int(m == 0))
                    for m in range(2):
                        down_tile(L, g, m, range(n - 1, n), int(m == 1))
                    for m in range(2, KD):
                        if m == KD - 1:
                            sum_mod(L, f"down{g}")
                        down_tile(L, g, m, range(n), 1)
            norm_sums(DEPTH, 0)

        @block.scalar
        def _(act):
            A = nc.scalar.activation

            prepared = [0]

            def prepare(func):
                n = prepared[0]
                prepared[0] += 1
                A(unread[:, n:n + 1], eps[:], func)

            def root_of_norm(n_full, n):
                act.wait_ge(full[6], n_full)
                A(root[:], ps[:, 6, 0:TT], ACT.Sqrt, bias=eps[:], scale=1.0 / D_MODEL)
                nc.scalar.drain()
                act.sem_inc(free[6], 1)
                act.sem_inc(root_ready, 1)

            def make_h(L, half):
                sh, sc = (SHIFT_A, SCALE_A) if half == 0 else (SHIFT_F, SCALE_F)
                act.wait_ge(mod_ready, max(ADA_NUMBER[(L, sc)], ADA_NUMBER.get((L, sh), 0)) + 2)
                for k in range(KD):
                    n = 16 * L + 8 * half + k
                    act.wait_ge(xn_ready, n + 1)
                    if n >= 2:
                        act.wait_ge(h_ready, n - 1)
                    for s in range(NSEQ):
                        c = slice(s * SEQ, (s + 1) * SEQ)
                        A(hf[:, k % 2, c], xn[:, k % 2, c], ACT.Identity, bias=mod[:, sh, k, s:s + 1],
                          scale=mod[:, sc, k, s:s + 1])
                    nc.scalar.drain()
                    nc.scalar.copy(h_hi[:, k, :], hf[:, k % 2, :]).then_inc(h_hi_ready, 1)

            def square_x(k, n):
                A(sq_x[:, n % 2, :], x[:, k, :], ACT.Square).then_inc(sq_ready, 1)

            def hi_slot(j, n, landed):
                act.wait_ge(slot_free, n + 1)
                act.wait_ge(raw_landed[j], landed)
                nc.scalar.copy(w_hi[:, j, :], w_raw[:, j, :]).then_inc(hi_done, 1)

            def split_hi(L, s):
                n = L * SLOTS + s
                if n < DEPTH * SLOTS:
                    hi_slot(n % RING, n, 16 * (n // RING + 1))

            def stats(g, s):
                for t in (2 * s, 2 * s + 1):
                    A(junk_o[:], o_sb[:, t, 512 * g:512 * g + 512], ACT.Square, scale=512 ** -0.5,
                      accum_out=st_o[:, 0, 2 * t + g:2 * t + g + 1])
                    nc.scalar.drain()

            def group_root(g):
                A(st_o[:, 1, g::2], st_o[:, 0, g::2], ACT.Sqrt, bias=eps[:]).then_inc(o_root, 1)

            def output_hi(L, k):
                wait_full(act, L, ("ot", k))
                A(h_hi[:, k, :], ps[:, k % 4, :], ACT.Identity,
                  scale=par[:, L, PC_GOUT + k:PC_GOUT + k + 1]).then_inc(ot_hi_ready, 1)

            act.wait_ge(c_landed, 16)
            A(cact[:], cact[:], ACT.Silu).then_inc(c_ready, 1)
            act.wait_ge(loaded, 16 * N_LOADS)
            act.wait_ge(const_ready, 1)
            for k in range(KD):
                if k >= 2:
                    act.wait_ge(sq_q, k - 1)
                square_x(k, k)
            for b in range(2):
                act.wait_ge(full[b], 1)
                nc.scalar.copy(shift_row[:, b * 512:(b + 1) * 512], ps[0:NSEQ, b, :])
            nc.scalar.drain()
            act.sem_inc(row_ready, 1)
            for b in range(2):
                act.sem_inc(free[b], 1)
            for s in range(3):
                split_hi(0, s)

            for L in range(DEPTH):
                root_of_norm(n_use(L, "norm1") + 1, 2 * L)
                make_h(L, 0)
                split_hi(L, 3)
                for c, (col, width) in enumerate(CHUNKS):
                    for t in range(TT):
                        wait_full(act, L, ("proj", c, t))
                        nc.scalar.copy(proj[:, t, col:col + width], ps[:, t, 0:width]).then_inc(free[t], 1)
                    if c == 1:
                        nc.scalar.drain()
                        for t in range(TT):
                            A(junk[:, 0:Q_LORA], proj[:, t, C_CQ:C_CQ + Q_LORA], ACT.Square, scale=Q_LORA ** -0.5,
                              accum_out=st_lat[:, 0, t:t + 1])
                            nc.scalar.drain()
                            A(junk[:, 0:KV_LORA], proj[:, t, C_CKV:C_CKV + KV_LORA], ACT.Square,
                              scale=KV_LORA ** -0.5, accum_out=st_lat[:, 0, 4 + t:5 + t])
                            nc.scalar.drain()
                        A(st_lat[:, 1, :], st_lat[:, 0, :], ACT.Sqrt, bias=eps[:]).then_inc(lat_sq, 1)
                    if c >= 2:
                        w, h0, nh = QK_BLOCKS[c - 2]
                        n = len(QK_BLOCKS) * L + c - 2
                        nc.scalar.drain()
                        A(sq_qk[:, :, 0:nh * HD], proj[:, :, C_Q + h0 * HD:C_Q + (h0 + nh) * HD],
                          ACT.Square).then_inc(qk_sq, 1)
                        act.wait_ge(qk_ms, n + 1)
                        A(qk_stat(1, h0, nh), qk_stat(0, h0, nh), ACT.Sqrt, bias=eps[:],
                          scale=1.0 / HD).then_inc(qk_root, 1)
                    if c == len(CHUNKS) - 2:
                        for j in range(3):
                            wait_full(act, L, ("lat", j))
                            A(ct_hi[:, j, :], ps[:, 4 + j, :], ACT.Identity,
                              scale=par[:, L, PC_GCQ + j:PC_GCQ + j + 1]).then_inc(ct_hi_ready, 1)
                    if c < len(CHUNKS) - 1:
                        for s in range(2):
                            split_hi(L, 2 * c + 4 + s)
                for s in range(2):
                    split_hi(L, S_UQ + 2 + s)
                for s in range(4):
                    for t in range(TT):
                        wait_full(act, L, ("uq", s, t))
                        nc.scalar.copy(qb[:, t, 2 * s:2 * s + 2, :],
                                       ps[:, t, 0:2 * QK_B].rearrange("p (h d) -> p h d", h=2)).then_inc(free[t], 1)
                    split_hi(L, S_UQ + 4 + s)
                for s in range(2):
                    for t in range(TT):
                        wait_full(act, L, ("ukv", s, t))
                        if s == 0:
                            nc.scalar.copy(kb[:, t, :, 0:NOPE],
                                           ps[:, t, :].rearrange("p (h d) -> p h d", h=HEADS)).then_inc(free[t], 1)
                        else:
                            nc.scalar.copy(vb[:, t, :], ps[:, t, :]).then_inc(free[t], 1)
                    if s == 0:
                        split_hi(L, S_UKV + 4)
                prepare(ACT.Exp)
                wait_full(act, L, "kat")
                nc.scalar.copy(ka_t[:], ps[:, 7, :])
                nc.scalar.drain()
                act.sem_inc(free[7], 1)
                act.sem_inc(ka_ready, 1)
                for i in range(-1, NU):
                    if i + 1 < NU and UNITS[i + 1][3]:
                        u = i + 1
                        b, buf = bank(("qt", u)), QT_BUF(u)
                        wait_full(act, L, ("qt", u))
                        last_reader = QT_LAST_READER(u)
                        if last_reader is not None:
                            wait_full(act, L, ("s", last_reader))
                        if UNITS[u][0] == "a":
                            nc.scalar.copy(qk_t[:, buf, 0:SEQ], ps[:, b, 0:SEQ])
                        else:
                            nc.scalar.copy(qk_t[0:QK_B, buf, :], ps[0:QK_B, b, :])
                        nc.scalar.drain()
                        act.sem_inc(free[b], 1)
                        act.sem_inc(qt_ready, 1)
                    if i >= 0:
                        d = HD if UNITS[i][0] == "a" else QK_B
                        act.wait_ge(max_ready, L * NU + i + 1)
                        if i >= 3:
                            wait_full(act, L, ("pt", i - 3))
                        for q in range(2):
                            A(prob[:, i % 3, q, :], ps[:, i % 3, q * SEQ:(q + 1) * SEQ], ACT.Exp,
                              bias=nmx[:, i, q:q + 1], scale=d ** -0.5, accum_out=sme[:, i, q:q + 1])
                        nc.scalar.drain()
                        act.sem_inc(free[i % 3], 1)
                        act.sem_inc(exp_ready, 1)
                        if i in STATS_AT_UNIT:
                            g, s = STATS_AT_UNIT[i]
                            key = ("o", 16 * g + 8 * s + 7)
                            act.wait_ge(free[bank(key)], n_use(L, key) + 1)
                            stats(g, s)
                            if (g, s) == (0, NSEQ - 1):
                                group_root(0)
                prepare(ACT.Sqrt)
                for k in range(LAG_O):
                    output_hi(L, k)
                act.wait_ge(free[bank(("o", NU - 1))], n_use(L, ("o", NU - 1)) + 1)
                stats(1, 1)
                group_root(1)
                for k in range(LAG_O, KD):
                    output_hi(L, k)
                split_hi(L, S_WO + 3)
                for m in range(KD):
                    n = KD + 2 * KD * L + m
                    act.wait_ge(x_upd, 2 * KD * L + m + 1)
                    act.wait_ge(sq_q, n - 1)
                    square_x(m, n)
                    if m < KD - 1:
                        split_hi(L, S_WO + 4 + m)
                root_of_norm(n_use(L, "norm2") + 1, 2 * L + 1)
                prepare(ACT.Silu)
                make_h(L, 1)
                split_hi(L, S_WO + 4 + KD - 1)
                for g, n in enumerate(GROUPS):
                    first = sum(GROUPS[:g])
                    with act.Fori(0, n // 2) as it:
                        for e in range(2):
                            tile = L * FT + first + e
                            for half in range(2):
                                ft = 2 * it + (half * FT + first + e)
                                key = ("up", g, e, half)
                                act.wait_ge(full[bank(key)], it + (n_use(L, key) + 1))
                                A(u_sb[:, e, half, :], ps[:, bank(key), :], ACT.Identity,
                                  bias=par[:, L, bass.ds(ft + PC_CB, 1)],
                                  scale=par[:, L, bass.ds(ft + (PC_CW + 2 * FT), 1)]).then_inc(mid_tap, 1)
                            act.wait_ge(taps_done, 2 * it + (tile + 1))
                            A(sil[:, e, :], u_sb[:, e, 1, :], ACT.Silu).then_inc(sil_ready, 1)
                            act.wait_ge(af_ready, 2 * it + (tile + 1))
                            nc.scalar.copy(a_hi[:, bass.ds(2 * it + e, 1), :], af[:, e:e + 1, :]).then_inc(a_hi_ready, 1)
                            for half in range(2):
                                n0 = L * SLOTS + S_UP[g] + 4 + 2 * e + half
                                hi_slot(n0 % RING, RING * it + n0, 16 * it + 16 * (n0 // RING + 1))
                    if g < len(GROUPS) - 1:
                        with act.Fori(0, KD // 4) as it:
                            for e in range(4):
                                n0 = L * SLOTS + S_DOWN[g] + 4 + e
                                hi_slot(n0 % RING, RING * it + n0, 16 * it + 16 * (n0 // RING + 1))
                    else:
                        for m in range(KD):
                            if m < KD - 1:
                                split_hi(L, S_DOWN[g] + 4 + m)
                            if m == KD - 1:
                                prepare(ACT.Sqrt)
                            n = KD + 2 * KD * L + KD + m
                            act.wait_ge(x_upd, 2 * KD * L + KD + m + 1)
                            act.wait_ge(sq_q, n - 1)
                            square_x(m, n)
            root_of_norm(USES[6] + 1, 2 * DEPTH)

        @block.vector
        def _(dve):
            V = nc.vector

            def ada_number(L, stage):
                return ADA_NUMBER[stage_vectors(L)[stage]]

            def ada_slots_of(L, stage, kts):
                if stage not in stage_vectors(L):
                    return
                n = ada_number(L, stage)
                for kt in kts:
                    if kt == 0:
                        ada_start(n)
                    ada_slot(n, kt)

            def ada_start(n):
                if n >= 1:
                    dve.wait_ge(mod_ready, n + 1)
                V.memset(ada_acc[:], 0.0)
                V.drain()

            def ada_slot(n, kt):
                dve.wait_ge(ada_landed[kt % 4], 16 * (2 * n + kt // 4 + 1))
                for s in range(NSEQ):
                    V.scalar_tensor_tensor(out=ada_acc[:, s, :], in0=ada_raw[:, kt % 4, :], scalar=cact[:, kt, s:s + 1],
                                           in1=ada_acc[:, s, :], op0=ALU.mult, op1=ALU.add)
                V.drain()
                dve.sem_inc(ada_used, 1)
                if kt == KD - 1:
                    dve.sem_inc(acc_ready, 1)

            def ada_finish(L, stage):
                if stage in stage_vectors(L):
                    dve.wait_ge(full[7], n_use(L, ("mod", stage)) + 1)
                    finish(*stage_vectors(L)[stage])

            def finish(L, v):
                bias = par[:, L, PC_BADA + v * KD:PC_BADA + (v + 1) * KD]
                V.tensor_tensor(mod[:, v, :, :], ps[:, 7, 0:2 * KD].rearrange("p (k s) -> p k s", s=2),
                                bias.rearrange("p (k o) -> p k o", o=1).broadcast_to([P, KD, NSEQ]), ALU.add)
                V.drain()
                if v in (SCALE_A, SCALE_F):
                    g0 = PC_GATTN if v == SCALE_A else PC_GFFN
                    V.tensor_scalar(mod[:, v, :, :], mod[:, v, :, :], 1.0, None, ALU.add)
                    V.drain()
                    V.tensor_tensor(mod[:, v, :, :], mod[:, v, :, :],
                                    par[:, L, g0:g0 + KD].rearrange("p (k o) -> p k o", o=1).broadcast_to([P, KD, NSEQ]),
                                    ALU.mult)
                    V.drain()
                dve.sem_inc(free[7], 1)
                dve.sem_inc(mod_ready, 1)

            def root_diagonals(n):
                dve.wait_ge(root_ready, n + 1)
                V.reciprocal(rstd[:], root[:])
                V.drain()
                for t in range(TT):
                    V.tensor_scalar(rstd_diag[:, t, :], ident[:], rstd[:, t:t + 1], None, ALU.mult)
                V.drain()
                dve.sem_inc(diag_ready, 1)

            def normalise(L, half):
                root_diagonals(2 * L + half)
                wait_full(dve, L, f"rstd{half + 1}")

                def lo(k):
                    n = 16 * L + 8 * half + k
                    dve.wait_ge(h_hi_ready, n + 1)
                    V.tensor_tensor(h_lo[:, k, :], hf[:, k % 2, :], h_hi[:, k, :].bitcast(F32),
                                    ALU.subtract).then_inc(h_ready, 1)

                for k in range(KD):
                    V.tensor_tensor(xn[:, k % 2, :], x[:, k, :], ps[:, 6, :], ALU.mult).then_inc(xn_ready, 1)
                    if k == KD - 1:
                        V.drain()
                        dve.sem_inc(free[6], 1)
                    if k >= 1:
                        lo(k - 1)
                lo(KD - 1)

            def normalise_group(L, g):
                dve.wait_ge(o_root, 2 * L + g + 1)
                V.reciprocal(st_o[:, 0, g::2], st_o[:, 1, g::2])
                V.drain()
                for t in range(TT):
                    o = o_sb[:, t, 512 * g:512 * g + 512]
                    V.tensor_scalar(o, o, st_o[:, 0, 2 * t + g:2 * t + g + 1], None, ALU.mult)
                V.drain()
                dve.sem_inc(o_ready, 1)

            def output_lo(L, k):
                dve.wait_ge(ot_hi_ready, KD * L + k + 1)
                V.scalar_tensor_tensor(out=h_lo[:, k, :], in0=ps[:, k % 4, :],
                                       scalar=par[:, L, PC_GOUT + k:PC_GOUT + k + 1],
                                       in1=h_hi[:, k, :].bitcast(F32), op0=ALU.mult, op1=ALU.subtract)
                V.drain()
                dve.sem_inc(free[k % 4], 1)
                dve.sem_inc(ot_ready, 1)

            def add_square(n):
                dve.wait_ge(sq_ready, n + 1)
                V.tensor_tensor(ssum[:], ssum[:], sq_x[:, n % 2, :], ALU.add)
                V.drain()
                dve.sem_inc(sq_q, 1)

            def update_x(L, key, k, v, plus=0, done=True):
                wait_full(dve, L, key, plus)
                for s in range(NSEQ):
                    c = slice(s * SEQ, (s + 1) * SEQ)
                    if type(k) is int:
                        xs, gate = x[:, k, c], mod[:, v, k, s:s + 1]
                    else:
                        xs, gate = x[:, bass.ds(k, 1), c], mod[:, v, bass.ds(k, 1), s]
                    V.scalar_tensor_tensor(out=xs, in0=ps[:, bank(key), c], scalar=gate, in1=xs,
                                           op0=ALU.mult, op1=ALU.add)
                V.drain()
                dve.sem_inc(free[bank(key)], 1)
                if done:
                    dve.sem_inc(x_upd, 1)

            dve.sem_inc(ada_used, 4)
            dve.wait_ge(c_ready, 1)
            V.memset(ssum[:], 0.0)
            ada_start(0)
            for kt in range(KD):
                ada_slot(0, kt)
            dve.wait_ge(const_ready, 1)
            for k in range(KD):
                add_square(k)
            dve.sem_inc(ssum_ready, 1)
            for n, v in enumerate((SHIFT_A, SCALE_A)):
                dve.wait_ge(full[7], n + 1)
                finish(0, v)

            for L in range(DEPTH):
                normalise(L, 0)
                for w in range(2):
                    g = gqk[:, L, w:w + 1, :]
                    V.tensor_tensor(cg[:, w], cos_a, g.broadcast_to([P, 2, HD]), ALU.mult)
                    for hf_ in range(2):
                        def quarter(ap, f):
                            return ap.rearrange("p e (s f d) -> p e s f d", s=2, f=2)[:, :, :, f, :]
                        V.tensor_tensor(quarter(sg_t[:, w], hf_), quarter(sin_a, hf_),
                                        quarter(g, 1 - hf_).broadcast_to([P, 2, 2, HD // 4]), ALU.mult)
                ada_slots_of(L, "in", range(0, 2))
                dve.wait_ge(lat_sq, L + 1)
                V.reciprocal(st_lat[:, 0, :], st_lat[:, 1, :])
                V.drain()
                for t in range(TT):
                    V.tensor_scalar(proj[:, t, C_CQ:C_CKV], proj[:, t, C_CQ:C_CKV], st_lat[:, 0, t:t + 1], None, ALU.mult)
                    V.tensor_scalar(proj[:, t, C_CKV:C_KR], proj[:, t, C_CKV:C_KR], st_lat[:, 0, 4 + t:5 + t], None,
                                    ALU.mult)
                V.drain()
                dve.sem_inc(lat_ready, 1)
                kr = proj[:, :, C_KR:C_KR + ROT]
                for e in range(2):
                    for f in range(2):
                        V.tensor_tensor(rot_view(kr_tmp[:, e::2, :], f), rot_view(kr[:, e::2, :], 1 - f),
                                        rot_view(sin_b[:, e:e + 1, :], f).broadcast_to([P, 2, 2, ROT // 4]), ALU.mult)
                for e in range(2):
                    V.tensor_tensor(kr_rot[:, e::2, :], kr[:, e::2, :], cos_b[:, e:e + 1, :].broadcast_to([P, 2, ROT]),
                                    ALU.mult)
                V.drain()
                V.tensor_tensor(kr_rot[:], kr_rot[:], kr_tmp[:], ALU.add).then_inc(kr_ready, 1)
                for n, (w, h0, nh) in enumerate(QK_BLOCKS, len(QK_BLOCKS) * L):
                    dve.wait_ge(qk_sq, n + 1)
                    V.tensor_reduce(out=qk_stat(0, h0, nh),
                                    in_=sq_qk[:, :, 0:nh * HD].rearrange("p t (h d) -> p t h d", d=HD),
                                    op=ALU.add, axis=AX_X)
                    V.drain()
                    dve.sem_inc(qk_ms, 1)
                    blk = proj[:, :, C_Q + h0 * HD:C_Q + (h0 + nh) * HD]
                    for t in range(TT):
                        for f in range(2):
                            def view(ap, f):
                                return ap.rearrange("p (h s f d) -> p h s f d", s=2, f=2, d=HD // 4)[:, :, :, f, :]
                            tb = sg_t[:, w, t % 2:t % 2 + 1, :].rearrange("p o (s f d) -> p o s f d", s=2, f=2)[:, :, :, f, :]
                            V.tensor_tensor(view(rope_tmp[:, t, 0:nh * HD], f), view(blk[:, t, :], 1 - f),
                                            tb.broadcast_to([P, nh, 2, HD // 4]), ALU.mult)
                    V.drain()
                    for t in range(TT):
                        xv = blk[:, t, :].rearrange("p (h d) -> p h d", d=HD)
                        V.tensor_tensor(xv, xv, cg[:, w, t % 2:t % 2 + 1, :].broadcast_to([P, nh, HD]), ALU.mult)
                    V.drain()
                    V.tensor_tensor(blk, blk, rope_tmp[:, :, 0:nh * HD], ALU.add)
                    dve.wait_ge(qk_root, n + 1)
                    V.reciprocal(qk_stat(0, h0, nh), qk_stat(1, h0, nh))
                    V.drain()
                    blk4 = blk.rearrange("p t (h d) -> p t h d", d=HD)
                    V.tensor_tensor(blk4, blk4, st_qk[:, 0, :].rearrange("p (t h o) -> p t h o", t=TT, o=1)[
                        :, :, h0:h0 + nh, :].broadcast_to([P, TT, nh, HD]), ALU.mult)
                    V.drain()
                    dve.sem_inc(qk_ready, 1)
                    if n % len(QK_BLOCKS) == 0:
                        ada_slots_of(L, "in", range(2, 3))
                    if n % len(QK_BLOCKS) == 1:
                        for j in range(3):
                            dve.wait_ge(ct_hi_ready, 3 * L + j + 1)
                            V.scalar_tensor_tensor(out=ct_lo[:, j, :], in0=ps[:, 4 + j, :],
                                                   scalar=par[:, L, PC_GCQ + j:PC_GCQ + j + 1],
                                                   in1=ct_hi[:, j, :].bitcast(F32), op0=ALU.mult, op1=ALU.subtract)
                            V.drain()
                            dve.sem_inc(free[4 + j], 1)
                            dve.sem_inc(ct_ready, 1)
                        ada_slots_of(L, "in", range(3, 4))
                ada_slots_of(L, "in", range(4, 8))
                ada_finish(L, "in")
                ada_slots_of(L, "attn", range(0, ADA_VECTOR_E))
                for i in range(NU + LAG_O):
                    if i < NU:
                        d = HD if UNITS[i][0] == "a" else QK_B
                        wait_full(dve, L, ("s", i))
                        V.tensor_reduce(out=mx[:, i, :], in_=ps[:, i % 3, :].rearrange("p (q k) -> p q k", q=2),
                                        op=ALU.max, axis=AX_X)
                        V.drain()
                        V.tensor_scalar(nmx[:, i, :], mx[:, i, :], -d ** -0.5, None, ALU.mult).then_inc(max_ready, 1)
                    if 0 <= i - LAG_P < NU:
                        u = i - LAG_P
                        wait_full(dve, L, ("pt", u))
                        if u >= 2:
                            wait_full(dve, L, ("o", u - 2))
                        V.tensor_copy(prob_t[:, u % 2, :, :], ps[:, 3, :].rearrange("p (a b) -> p a b", a=2))
                        V.reciprocal(rin[:, u, :], sme[:, u, :])
                        V.drain()
                        dve.sem_inc(free[3], 1)
                        dve.sem_inc(pt_ready, 1)
                    if 0 <= i - LAG_O < NU:
                        u = i - LAG_O
                        group, s, h, _ = UNITS[u]
                        b = bank(("o", u))
                        wait_full(dve, L, ("o", u))
                        col = h * HD + (512 if group == "b" else 0)
                        V.tensor_tensor(o_sb[:, 2 * s:2 * s + 2, col:col + HD],
                                        ps[:, b, 0:2 * HD].rearrange("p (q d) -> p q d", q=2),
                                        rin[:, u, :].rearrange("p (q o) -> p q o", o=1).broadcast_to([P, 2, HD]),
                                        ALU.mult).then_inc(free[b], 1)
                    if i == NORM_A_AT:
                        normalise_group(L, 0)
                    if i > NU:
                        output_lo(L, i - NU - 1)
                for k in range(LAG_O - 1, KD // 2 - 1):
                    output_lo(L, k)
                normalise_group(L, 1)
                for k in range(KD // 2 - 1, KD):
                    output_lo(L, k)
                ada_finish(L, "attn")
                V.memset(ssum[:], 0.0)
                V.drain()
                n_sq = KD + 2 * KD * L
                for m in range(KD):
                    update_x(L, ("wo", m), m, GATE_A)
                    if m >= 1:
                        add_square(n_sq + m - 1)
                    ada_slots_of(L, "wo", [m])
                add_square(n_sq + KD - 1)
                dve.sem_inc(ssum_ready, 1)
                ada_finish(L, "wo")
                normalise(L, 1)
                for g, n in enumerate(GROUPS):
                    first = sum(GROUPS[:g])

                    def tile(i, quad):
                        e = i % 2
                        at = 4 * quad + (first + i)
                        for half in range(2):
                            key = ("up", g, i, half)
                            b = bank(key)
                            dve.wait_ge(mid_tap, 8 * quad + (2 * (L * FT + first + i) + half + 1))
                            for tap, (dst, src) in ((0, (1, 0)), (2, (0, 1))):
                                u3 = u_sb[:, e, half, :].rearrange("p (s t) -> p s t", s=2)
                                p3 = ps[:, b, :].rearrange("p (s t) -> p s t", s=2)
                                V.scalar_tensor_tensor(
                                    out=u3[:, :, dst:dst + SEQ - 1], in0=p3[:, :, src:src + SEQ - 1],
                                    scalar=par[:, L, bass.ds(at + (PC_CW + tap * 2 * FT + half * FT), 1)],
                                    in1=u3[:, :, dst:dst + SEQ - 1], op0=ALU.mult, op1=ALU.add)
                                V.drain()
                            dve.sem_inc(free[b], 1)
                        dve.sem_inc(taps_done, 1)
                        dve.wait_ge(sil_ready, 4 * quad + (L * FT + first + i + 1))
                        V.tensor_tensor(af[:, e, :], sil[:, e, :], u_sb[:, e, 0, :], ALU.mult)
                        V.drain()
                        dve.sem_inc(af_ready, 1)
                        dve.wait_ge(a_hi_ready, 4 * quad + (L * FT + first + i + 1))
                        lo_at = bass.ds(4 * quad + i, 1)
                        V.tensor_tensor(a_lo[:, lo_at, :], af[:, e:e + 1, :], a_hi[:, lo_at, :].bitcast(F32),
                                        ALU.subtract).then_inc(a_ready, 1)

                    for i in range(n):
                        tile(i % 4, i // 4)
                        ada_slots_of(L, f"up{g}", ADA_AT_UP[g].get(i, ()))
                    ada_finish(L, f"up{g}")
                    if g == len(GROUPS) - 1:
                        V.memset(ssum[:], 0.0)
                        V.drain()
                    n_sq = 2 * KD + 2 * KD * L
                    for m in range(KD):
                        update_x(L, ("down", g, m), m, GATE_F, done=g == len(GROUPS) - 1)
                        if g == len(GROUPS) - 1 and m >= 1:
                            add_square(n_sq + m - 1)
                        ada_slots_of(L, f"down{g}", ADA_AT_DOWN[m])
                    ada_finish(L, f"down{g}")
                add_square(n_sq + KD - 1)
                dve.sem_inc(ssum_ready, 1)
            root_diagonals(2 * DEPTH)
            dve.wait_ge(full[6], USES[6] + 2)
            for k in range(KD):
                V.scalar_tensor_tensor(out=x[:, k, :], in0=x[:, k, :], scalar=gfin[:, k:k + 1], in1=ps[:, 6, :],
                                       op0=ALU.mult, op1=ALU.mult).then_inc(y_done, 1)


SHIFT0 = (DEPTH * N_MOD - 1) * KD

_BLOCKS = [u for u in range(NU) if UNITS[u][3]]


def _block_of(u):
    return max(n for n, first in enumerate(_BLOCKS) if first <= u)


def QT_BUF(u):
    return _block_of(u) % 2


def QT_DONE(L, u):
    return L * len(_BLOCKS) + _block_of(u) + 1


def QT_LAST_READER(u):
    n = _block_of(u)
    return _BLOCKS[n - 1] - 1 if n >= 2 else None


def _tables():
    out = []
    for d in (HD, ROT):
        q = d // 4
        t = np.arange(SEQ)
        pos = np.stack([t // GRID_W, t % GRID_W], -1).astype(np.float32)
        inv = np.float32(THETA) ** (-np.arange(q, dtype=np.float32) / np.float32(q))
        ang = (pos[:, :, None] * inv).astype(np.float32)
        c, s = np.cos(ang), np.sin(ang)
        cos = np.stack([c, c], 2).reshape(2, P, d).transpose(1, 0, 2).reshape(P, 2 * d)
        sin = np.stack([-s, s], 2).reshape(2, P, d).transpose(1, 0, 2).reshape(P, 2 * d)
        out.append(np.stack([cos, sin], 1))
    return np.ascontiguousarray(np.concatenate(out, -1), np.float32)


def _columns(v, n):
    return np.moveaxis(v.reshape(*v.shape[:-1], n, P), -1, 0)


def _pack(inp):
    f = {k: np.asarray(v) for k, v in inp.items()}
    xs = np.concatenate([f["x_prompt"].reshape(SEQ, D_MODEL), f["x_sample"].reshape(SEQ, D_MODEL)], 0)
    x_t = xs.T.reshape(KD, P, T).transpose(1, 0, 2)
    cs = np.concatenate([f["c_prompt"], f["c_sample"]], 0)
    c_t = cs.reshape(NSEQ, KD, P).transpose(2, 1, 0)
    ada = f["w_ada"].reshape(DEPTH, KD, P, N_MOD, SLOT).transpose(0, 3, 1, 2, 4).reshape(DEPTH * N_MOD * KD, P, SLOT)
    order = ORDER + [(0, SHIFT_A)]
    ada = ada.reshape(DEPTH, N_MOD, KD, P, SLOT)[[L for L, _ in order], [v for _, v in order]].reshape(-1, P, SLOT)
    slots = np.zeros((DEPTH, SLOTS, P, SLOT), np.float32)
    w_in = f["w_in"]
    wa, kva = HEADS * HD, KV_HEADS * HD
    order = []
    base_cq = wa + 2 * kva
    order += list(range(base_cq, base_cq + Q_LORA + KV_LORA + ROT))
    for p in range(4):
        for g in range(2):
            order += list(range((p + 4 * g) * HD, (p + 4 * g + 1) * HD))
    order += list(range(wa, wa + 2 * kva))
    w_in = w_in[:, :, order]
    for c, (col, width) in enumerate(CHUNKS):
        v = w_in[:, :, col:col + width].reshape(DEPTH, 2, 4, P, width).transpose(0, 1, 3, 2, 4)
        slots[:, S_IN + 2 * c:S_IN + 2 * c + 2, :, 0:4 * width] = v.reshape(DEPTH, 2, P, 4 * width)
    width = 2 * QK_B
    v = f["w_uq"].reshape(DEPTH, 2, P, 4, width).transpose(0, 3, 2, 1, 4)
    slots[:, S_UQ:S_UQ + 4, :, 0:2 * width] = v.reshape(DEPTH, 4, P, 2 * width)
    v = f["w_ukv"].reshape(DEPTH, P, HEADS, 2, HD).transpose(0, 3, 1, 2, 4)
    slots[:, S_UKV:S_UKV + 2, :, 0:HEADS * HD] = v.reshape(DEPTH, 2, P, HEADS * HD)

    def by_column_tile(w, k):
        n = w.shape[2] // P
        return w.reshape(DEPTH, k, P, n, P).transpose(0, 3, 2, 1, 4).reshape(DEPTH, n, P, k * P)

    slots[:, S_WO:S_WO + KD] = by_column_tile(f["w_o"], KD)
    up = by_column_tile(f["w_up"], KD)
    first = 0
    for g, n in enumerate(GROUPS):
        s = S_UP[g]
        slots[:, s:s + 2 * n:2] = up[:, first:first + n]
        slots[:, s + 1:s + 2 * n:2] = up[:, FT + first:FT + first + n]
        s = S_DOWN[g]
        slots[:, s:s + KD, :, 0:n * P] = by_column_tile(f["w_down"][:, first * P:(first + n) * P], n)
        first += n
    par = [_columns(f["g_attn"], KD), _columns(f["g_ffn"], KD),
           _columns(f["g_out_a"], KD // 2), _columns(f["g_out_b"], KD // 2),
           _columns(f["g_cq"], 2), _columns(f["g_ckv"], 1), _columns(f["b_ada"], N_MOD * KD),
           _columns(f["conv_w"], 2 * FT).reshape(P, DEPTH, 6 * FT), _columns(f["conv_b"], 2 * FT)]
    gqk = np.stack([f["g_q_a"], f["g_k_a"]], 1)
    ins = {
        "x_t": x_t, "c_t": c_t, "w_slots": slots.reshape(DEPTH * SLOTS, P, SLOT), "ada_slots": ada,
        "params": np.concatenate(par, -1), "g_qk": np.broadcast_to(gqk, (P, *gqk.shape)),
        "g_fin": _columns(f["g_final"], KD), "tables": _tables(), "ident": np.eye(P, dtype=np.float32),
    }
    return {k: np.ascontiguousarray(v) for k, v in ins.items()}


def kernel(**inputs):
    import concourse.bacc as bacc
    from concourse.bass_utils import run_bass_kernel_spmd

    arrays = _pack(inputs)
    nc = bacc.Bacc("TRN2", target_bir_lowering=False, num_devices=1)
    args = [nc.dram_tensor(k, v.shape, F32, kind="ExternalInput").ap() for k, v in arrays.items()]
    y = nc.dram_tensor("y_t", (P, KD, T), F32, kind="ExternalOutput").ap()
    encoder_kernel(nc, *args, y)
    r = run_bass_kernel_spmd(nc, [arrays], core_ids=[0])
    y = np.asarray(r.results[0]["y_t"]).transpose(2, 1, 0).reshape(NSEQ, SEQ, D_MODEL)
    return y[0:1], y[1:2]
```
